# Optimizing a Trainium2 kernel written in Bass

```python
import math
import jax, jax.numpy as jnp
from jax import lax
import numpy as np

D_MODEL = 1024
BATCH = 1
SEQ = 256
DEPTH = 1

CHUNK = 64
LEFT_CHUNKS = 8
BAND = LEFT_CHUNKS + 1
N_HEADS = 16
HEAD_DIM = 64
D_ATTN = N_HEADS * HEAD_DIM
MAX_REL = 128
D_RNN = D_MODEL
N_RG_BLOCKS = 16
RG_BLOCK = D_RNN // N_RG_BLOCKS
CONV_W = 4
RG_C = 8.0
D_FF = ((8 * D_MODEL // 3 + 255) // 256) * 256
IN_COLS = 3 * D_ATTN + 2 * D_RNN + 2 * D_MODEL
EPS = 1e-6
NEG_INF = -1e30


def rmsnorm(x, g):
    xf = x.astype(jnp.float32)
    var = jnp.mean(xf * xf, axis=-1, keepdims=True)
    return (xf * lax.rsqrt(var + EPS) * g.astype(jnp.float32)).astype(x.dtype)

def rel_bias_band(table):
    i = jnp.arange(CHUNK)[:, None]
    m = jnp.arange(BAND * CHUNK)[None, :]
    dist = i - m + LEFT_CHUNKS * CHUNK
    idx = jnp.clip(dist, -MAX_REL, MAX_REL) + MAX_REL
    return table[:, idx]

def chunked_band_attention(q, k, v, rel_table):
    B, S, _ = q.shape
    nc = S // CHUNK
    q = q.reshape(B, nc, CHUNK, N_HEADS, HEAD_DIM)
    k = k.reshape(B, nc, CHUNK, N_HEADS, HEAD_DIM)
    v = v.reshape(B, nc, CHUNK, N_HEADS, HEAD_DIM)
    pad = jnp.zeros((B, LEFT_CHUNKS, CHUNK, N_HEADS, HEAD_DIM), k.dtype)
    kp = jnp.concatenate([pad, k], axis=1)
    vp = jnp.concatenate([pad, v], axis=1)
    kb = jnp.concatenate([kp[:, j:j + nc] for j in range(BAND)], axis=2)
    vb = jnp.concatenate([vp[:, j:j + nc] for j in range(BAND)], axis=2)
    scale = 1.0 / math.sqrt(HEAD_DIM)
    s = jnp.einsum('bnqhd,bnkhd->bhnqk', q, kb).astype(jnp.float32) * scale
    s = s + rel_bias_band(rel_table).astype(jnp.float32)[None, :, None, :, :]
    key_chunk = jnp.arange(nc)[:, None] - LEFT_CHUNKS + (jnp.arange(BAND * CHUNK)[None, :] // CHUNK)
    valid = key_chunk >= 0
    s = jnp.where(valid[None, None, :, None, :], s, NEG_INF)
    p = jax.nn.softmax(s, axis=-1).astype(v.dtype)
    o = jnp.einsum('bhnqk,bnkhd->bnqhd', p, vb)
    return o.reshape(B, S, D_ATTN)

def causal_depthwise_conv(x, w, b):
    S = x.shape[1]
    xp = jnp.pad(x, ((0, 0), (CONV_W - 1, 0), (0, 0)))
    y = sum(xp[:, j:j + S] * w[j] for j in range(CONV_W))
    return y + b

def rg_lru(x, w_r, b_r, w_i, b_i, lam):
    B, S, D = x.shape
    xb = x.reshape(B, S, N_RG_BLOCKS, RG_BLOCK)
    r = jax.nn.sigmoid(jnp.einsum('bsnd,nde->bsne', xb, w_r).reshape(B, S, D) + b_r)
    i = jax.nn.sigmoid(jnp.einsum('bsnd,nde->bsne', xb, w_i).reshape(B, S, D) + b_i)
    log_a = -RG_C * r.astype(jnp.float32) * jax.nn.softplus(-lam.astype(jnp.float32))
    a = jnp.exp(log_a)
    mult = jnp.sqrt(-jnp.expm1(2.0 * log_a))
    bx = mult * (i * x).astype(jnp.float32)

    def combine(left, right):
        a1, b1 = left
        a2, b2 = right
        return a1 * a2, a2 * b1 + b2

    _, h = lax.associative_scan(combine, (a, bx), axis=1)
    return h.astype(x.dtype)

def first_inputs(seed: int = 0) -> dict:
    key = jax.random.key(seed)
    ks = jax.random.split(key, 20)
    L = DEPTH

    def nrm(k, shape, fan_in):
        return jax.random.normal(k, shape, jnp.float32) * (fan_in ** -0.5)

    x = jax.random.normal(ks[0], (BATCH, SEQ, D_MODEL), jnp.float32)
    norm_mix_g = 1.0 + 0.05 * jax.random.normal(ks[1], (L, D_MODEL), jnp.float32)
    w_in = nrm(ks[2], (L, D_MODEL, IN_COLS), D_MODEL)
    b_merge = 0.01 * jax.random.normal(ks[3], (L, 2 * D_MODEL), jnp.float32)
    rel_table = 0.5 * jax.random.normal(ks[4], (L, N_HEADS, 2 * MAX_REL + 1), jnp.float32)
    w_attn_out = nrm(ks[5], (L, D_ATTN, D_MODEL), D_ATTN)
    conv_w = nrm(ks[6], (L, CONV_W, D_RNN), CONV_W)
    conv_b = 0.01 * jax.random.normal(ks[7], (L, D_RNN), jnp.float32)
    w_rg_r = nrm(ks[8], (L, N_RG_BLOCKS, RG_BLOCK, RG_BLOCK), RG_BLOCK)
    b_rg_r = 0.01 * jax.random.normal(ks[9], (L, D_RNN), jnp.float32)
    w_rg_i = nrm(ks[10], (L, N_RG_BLOCKS, RG_BLOCK, RG_BLOCK), RG_BLOCK)
    b_rg_i = 0.01 * jax.random.normal(ks[11], (L, D_RNN), jnp.float32)
    u = jax.random.uniform(ks[12], (L, D_RNN), jnp.float32, 0.9, 0.999)
    a0 = u ** (1.0 / RG_C)
    rg_lambda = jnp.log(a0) - jnp.log1p(-a0)
    w_rnn_out = nrm(ks[13], (L, D_RNN, D_MODEL), D_RNN)
    w_o = nrm(ks[14], (L, D_MODEL, D_MODEL), D_MODEL)
    norm_ffn_g = 1.0 + 0.05 * jax.random.normal(ks[15], (L, D_MODEL), jnp.float32)
    w_ffn_in = nrm(ks[16], (L, D_MODEL, 2 * D_FF), D_MODEL)
    w_ffn_out = nrm(ks[17], (L, D_FF, D_MODEL), D_FF)
    final_norm_g = 1.0 + 0.05 * jax.random.normal(ks[18], (D_MODEL,), jnp.float32)
    return {"x": x, "norm_mix_g": norm_mix_g, "w_in": w_in, "b_merge": b_merge,
            "rel_table": rel_table, "w_attn_out": w_attn_out, "conv_w": conv_w,
            "conv_b": conv_b, "w_rg_r": w_rg_r, "b_rg_r": b_rg_r, "w_rg_i": w_rg_i,
            "b_rg_i": b_rg_i, "rg_lambda": rg_lambda, "w_rnn_out": w_rnn_out, "w_o": w_o,
            "norm_ffn_g": norm_ffn_g, "w_ffn_in": w_ffn_in, "w_ffn_out": w_ffn_out,
            "final_norm_g": final_norm_g}

def first_block(x, norm_mix_g, w_in, b_merge, rel_table, w_attn_out, conv_w, conv_b,
              w_rg_r, b_rg_r, w_rg_i, b_rg_i, rg_lambda, w_rnn_out, w_o,
              norm_ffn_g, w_ffn_in, w_ffn_out, final_norm_g):
    h = x
    splits = [D_ATTN, 2 * D_ATTN, 3 * D_ATTN, 3 * D_ATTN + D_RNN,
              3 * D_ATTN + 2 * D_RNN, 3 * D_ATTN + 2 * D_RNN + D_MODEL]
    for l in range(DEPTH):
        xn = rmsnorm(h, norm_mix_g[l])
        u = jnp.einsum('bsd,de->bse', xn, w_in[l])
        q, k, v, xr, gr, ga, gb = jnp.split(u, splits, axis=-1)
        ya = chunked_band_attention(q, k, v, rel_table[l]) @ w_attn_out[l]
        xc = causal_depthwise_conv(xr, conv_w[l], conv_b[l])
        hr = rg_lru(xc, w_rg_r[l], b_rg_r[l], w_rg_i[l], b_rg_i[l], rg_lambda[l])
        yb = (hr * jax.nn.gelu(gr)) @ w_rnn_out[l]
        gates = jax.nn.sigmoid(jnp.concatenate([ga, gb], axis=-1) + b_merge[l])
        g_a, g_b = jnp.split(gates, 2, axis=-1)
        h = h + (g_a * ya + g_b * yb) @ w_o[l]
        hn = rmsnorm(h, norm_ffn_g[l])
        gu = hn @ w_ffn_in[l]
        g, up = jnp.split(gu, 2, axis=-1)
        h = h + (jax.nn.silu(g) * up) @ w_ffn_out[l]
    return rmsnorm(h, final_norm_g)


DEPTH_2 = 2

N_MIXERS = 2
DN_HEADS = 8
DN_HEAD_DIM = 128
DN_DIM = DN_HEADS * DN_HEAD_DIM
DN_CONV = 4
DN_CHUNK = 64
DN_IN = 4 * DN_DIM + 2 * DN_HEADS
MB_HEADS = 8
MB_HEAD_DIM = D_MODEL // MB_HEADS
MB_DIM = MB_HEADS * MB_HEAD_DIM
MB_BLOCK = 256
MB_TOPK = 3
MB_QCHUNK = 16
D_FF_2 = 4 * D_MODEL
RMS_EPS = 1e-6
N_DN_LAYERS = (DEPTH_2 + 1) // 2
N_MB_LAYERS = DEPTH_2 // 2


def rmsnorm_2(x, g):
    xf = x.astype(jnp.float32)
    y = xf * lax.rsqrt(jnp.mean(xf * xf, axis=-1, keepdims=True) + RMS_EPS)
    return (y * g.astype(jnp.float32)).astype(x.dtype)

def l2norm(x):
    xf = x.astype(jnp.float32)
    return xf * lax.rsqrt(jnp.sum(xf * xf, axis=-1, keepdims=True) + 1e-6)

def causal_depthwise_conv_2(x, w):
    k_w = w.shape[0]
    t = x.shape[1]
    xp = jnp.pad(x, ((0, 0), (k_w - 1, 0), (0, 0)))
    y = xp[:, 0:t] * w[0]
    for j in range(1, k_w):
        y = y + xp[:, j:j + t] * w[j]
    return y

def alibi_slopes(n_heads):
    return jnp.exp2(-8.0 * jnp.arange(1, n_heads + 1, dtype=jnp.float32) / n_heads)

def chunk_gated_delta_rule(q, k, v, g, beta):
    b, h, t, dk = q.shape
    dv = v.shape[-1]
    c = DN_CHUNK
    n = t // c
    q = q.astype(jnp.float32).reshape(b, h, n, c, dk)
    k = k.astype(jnp.float32).reshape(b, h, n, c, dk)
    v = v.astype(jnp.float32).reshape(b, h, n, c, dv)
    g = g.astype(jnp.float32).reshape(b, h, n, c)
    beta = beta.astype(jnp.float32).reshape(b, h, n, c)

    gc = jnp.cumsum(g, axis=-1)
    idx = jnp.arange(c)
    tri_incl = idx[:, None] >= idx[None, :]
    tri_strict = idx[:, None] > idx[None, :]
    decay = jnp.exp(jnp.where(tri_incl, gc[..., :, None] - gc[..., None, :], -jnp.inf))

    k_beta = k * beta[..., None]
    a_low = jnp.where(tri_strict, jnp.einsum('bhncd,bhnsd->bhncs', k_beta, k) * decay, 0.0)
    a_mat = a_low + jnp.eye(c, dtype=jnp.float32)
    rhs = jnp.concatenate([v * beta[..., None], k_beta * jnp.exp(gc)[..., None]], axis=-1)
    sol = lax.linalg.triangular_solve(a_mat, rhs, left_side=True, lower=True, unit_diagonal=True)
    u, w = sol[..., :dv], sol[..., dv:]

    attn_intra = jnp.einsum('bhncd,bhnsd->bhncs', q, k) * decay
    q_dec = q * jnp.exp(gc)[..., None]
    k_dec = k * jnp.exp(gc[..., -1:] - gc)[..., None]
    g_tot = jnp.exp(gc[..., -1])

    xs = tuple(jnp.moveaxis(a, 2, 0) for a in (u, w, q_dec, k_dec, attn_intra, g_tot))

    def step(state, inp):
        u_c, w_c, qd_c, kd_c, at_c, gt_c = inp
        v_new = u_c - jnp.einsum('bhcd,bhde->bhce', w_c, state)
        o_c = jnp.einsum('bhcd,bhde->bhce', qd_c, state) + jnp.einsum('bhcs,bhse->bhce', at_c, v_new)
        state = state * gt_c[..., None, None] + jnp.einsum('bhcd,bhce->bhde', kd_c, v_new)
        return state, o_c

    s0 = jnp.zeros((b, h, dk, dv), jnp.float32)
    _, o = lax.scan(step, s0, xs)
    return jnp.moveaxis(o, 0, 2).reshape(b, h, t, dv)

def gated_deltanet(hn, w_in, conv_w, a_log, dt_bias, out_norm_g, w_out):
    b, t, _ = hn.shape
    proj = hn @ w_in
    qkv = jax.nn.silu(causal_depthwise_conv_2(proj[..., :3 * DN_DIM], conv_w))
    z = proj[..., 3 * DN_DIM:4 * DN_DIM]
    b_raw = proj[..., 4 * DN_DIM:4 * DN_DIM + DN_HEADS].astype(jnp.float32)
    a_raw = proj[..., 4 * DN_DIM + DN_HEADS:].astype(jnp.float32)

    def heads(a):
        return a.reshape(b, t, DN_HEADS, DN_HEAD_DIM).transpose(0, 2, 1, 3)

    q = heads(l2norm(heads(qkv[..., :DN_DIM]).transpose(0, 2, 1, 3)) * DN_HEAD_DIM ** -0.5)
    k = heads(l2norm(heads(qkv[..., DN_DIM:2 * DN_DIM]).transpose(0, 2, 1, 3)))
    v = heads(qkv[..., 2 * DN_DIM:])
    beta = jax.nn.sigmoid(b_raw).transpose(0, 2, 1)
    g = (-jnp.exp(a_log.astype(jnp.float32)) *
         jax.nn.softplus(a_raw + dt_bias.astype(jnp.float32))).transpose(0, 2, 1)
    o = chunk_gated_delta_rule(q, k, v, g, beta)
    o = o.transpose(0, 2, 1, 3).astype(hn.dtype)
    o = rmsnorm_2(o, out_norm_g) * jax.nn.silu(z.reshape(b, t, DN_HEADS, DN_HEAD_DIM))
    return o.reshape(b, t, DN_DIM) @ w_out

def moba_attention(q, k, v):
    b, h, t, dh = q.shape
    nb = -(-t // MB_BLOCK)
    tp = nb * MB_BLOCK
    pad = ((0, 0), (0, 0), (0, tp - t), (0, 0))
    q, k, v = jnp.pad(q, pad), jnp.pad(k, pad), jnp.pad(v, pad)
    kb = k.reshape(b, h, nb, MB_BLOCK, dh)
    vb = v.reshape(b, h, nb, MB_BLOCK, dh)
    top = min(MB_TOPK, nb)
    scale = dh ** -0.5
    slopes = alibi_slopes(h)

    k_mean = jnp.mean(kb.astype(jnp.float32), axis=3)
    gate = jnp.einsum('bhtd,bhnd->bhtn', q.astype(jnp.float32), k_mean)
    q_blk = jnp.arange(tp) // MB_BLOCK
    past = jnp.arange(nb)[None, :] < q_blk[:, None]
    gate = jnp.where(past, gate, -jnp.inf)
    _, sel = lax.top_k(gate, top)
    valid = sel < q_blk[:, None]

    n_qc = tp // MB_QCHUNK

    def to_chunks(a):
        return jnp.moveaxis(a.reshape(b, h, n_qc, MB_QCHUNK, *a.shape[3:]), 2, 0)

    gather_blocks = jax.vmap(jax.vmap(lambda blocks, ids: blocks[ids]))

    def attend_chunk(args):
        qc, selc, validc, ci = args
        t0 = ci * MB_QCHUNK
        blk = t0 // MB_BLOCK
        tpos = (t0 + jnp.arange(MB_QCHUNK)).astype(jnp.float32)
        ks = gather_blocks(kb, selc)
        vs = gather_blocks(vb, selc)
        s_sel = jnp.einsum('bhqd,bhqnld->bhqnl', qc, ks).astype(jnp.float32) * scale
        kpos_sel = (selc[..., None] * MB_BLOCK + jnp.arange(MB_BLOCK)).astype(jnp.float32)
        dist_sel = tpos[:, None, None] - kpos_sel
        s_sel = jnp.where(validc[..., None], s_sel - slopes[:, None, None, None] * dist_sel, -jnp.inf)
        ko = lax.dynamic_index_in_dim(kb, blk, axis=2, keepdims=False)
        vo = lax.dynamic_index_in_dim(vb, blk, axis=2, keepdims=False)
        s_own = jnp.einsum('bhqd,bhld->bhql', qc, ko).astype(jnp.float32) * scale
        dist_own = tpos[:, None] - (blk * MB_BLOCK + jnp.arange(MB_BLOCK)).astype(jnp.float32)
        s_own = jnp.where(dist_own >= 0, s_own - slopes[:, None, None] * dist_own, -jnp.inf)
        logits = jnp.concatenate([s_sel.reshape(b, h, MB_QCHUNK, top * MB_BLOCK), s_own], axis=-1)
        p = jax.nn.softmax(logits, axis=-1).astype(vs.dtype)
        p_sel = p[..., :top * MB_BLOCK].reshape(b, h, MB_QCHUNK, top, MB_BLOCK)
        p_own = p[..., top * MB_BLOCK:]
        return (jnp.einsum('bhqnl,bhqnld->bhqd', p_sel, vs) +
                jnp.einsum('bhql,bhld->bhqd', p_own, vo))

    out = lax.map(attend_chunk, (to_chunks(q), to_chunks(sel), to_chunks(valid), jnp.arange(n_qc)))
    out = jnp.moveaxis(out, 0, 2).reshape(b, h, tp, dh)
    return out[:, :, :t]

def moba_layer(hn, w_in, w_out):
    b, t, _ = hn.shape
    proj = hn @ w_in

    def heads(a):
        return a.reshape(b, t, MB_HEADS, MB_HEAD_DIM).transpose(0, 2, 1, 3)

    q = heads(proj[..., :MB_DIM])
    k = heads(proj[..., MB_DIM:2 * MB_DIM])
    v = heads(proj[..., 2 * MB_DIM:])
    o = moba_attention(q, k, v)
    return o.transpose(0, 2, 1, 3).reshape(b, t, MB_DIM) @ w_out

def squared_relu_mlp(hn, w_up, w_down):
    return jnp.square(jax.nn.relu(hn @ w_up)) @ w_down

def second_inputs(seed: int = 0) -> dict:
    key = jax.random.key(seed)
    ks = jax.random.split(key, 16)
    f32 = jnp.float32
    x = jax.random.normal(ks[0], (BATCH, SEQ, D_MODEL), f32)
    mix_norm_g = 1.0 + 0.02 * jax.random.normal(ks[1], (DEPTH_2, D_MODEL), f32)
    mlp_norm_g = 1.0 + 0.02 * jax.random.normal(ks[2], (DEPTH_2, D_MODEL), f32)
    dn_w_in = jax.random.normal(ks[3], (N_DN_LAYERS, D_MODEL, DN_IN), f32) * D_MODEL ** -0.5
    dn_conv_w = jax.random.normal(ks[4], (N_DN_LAYERS, DN_CONV, 3 * DN_DIM), f32) * DN_CONV ** -0.5
    dn_a_log = jnp.log(jax.random.uniform(ks[5], (N_DN_LAYERS, DN_HEADS), f32, 1.0, 16.0))
    dt = jnp.exp(jax.random.uniform(ks[6], (N_DN_LAYERS, DN_HEADS), f32, math.log(1e-3), math.log(1e-1)))
    dn_dt_bias = dt + jnp.log(-jnp.expm1(-dt))
    dn_out_norm_g = 1.0 + 0.02 * jax.random.normal(ks[7], (N_DN_LAYERS, DN_HEAD_DIM), f32)
    dn_w_out = jax.random.normal(ks[8], (N_DN_LAYERS, DN_DIM, D_MODEL), f32) * DN_DIM ** -0.5
    mb_w_in = jax.random.normal(ks[9], (N_MB_LAYERS, D_MODEL, 3 * MB_DIM), f32) * D_MODEL ** -0.5
    mb_w_out = jax.random.normal(ks[10], (N_MB_LAYERS, MB_DIM, D_MODEL), f32) * MB_DIM ** -0.5
    mlp_w_up = jax.random.normal(ks[11], (DEPTH_2, D_MODEL, D_FF_2), f32) * D_MODEL ** -0.5
    mlp_w_down = jax.random.normal(ks[12], (DEPTH_2, D_FF_2, D_MODEL), f32) * D_FF_2 ** -0.5
    final_norm_g = 1.0 + 0.02 * jax.random.normal(ks[13], (D_MODEL,), f32)
    return {"x": x, "mix_norm_g": mix_norm_g, "mlp_norm_g": mlp_norm_g,
            "dn_w_in": dn_w_in, "dn_conv_w": dn_conv_w, "dn_a_log": dn_a_log,
            "dn_dt_bias": dn_dt_bias, "dn_out_norm_g": dn_out_norm_g, "dn_w_out": dn_w_out,
            "mb_w_in": mb_w_in, "mb_w_out": mb_w_out,
            "mlp_w_up": mlp_w_up, "mlp_w_down": mlp_w_down, "final_norm_g": final_norm_g}

def second_block(x, mix_norm_g, mlp_norm_g, dn_w_in, dn_conv_w, dn_a_log, dn_dt_bias,
              dn_out_norm_g, dn_w_out, mb_w_in, mb_w_out, mlp_w_up, mlp_w_down, final_norm_g):
    h = x
    for i in range(DEPTH_2):
        hn = rmsnorm_2(h, mix_norm_g[i])
        j = i // N_MIXERS
        if i % N_MIXERS == 0:
            mix = gated_deltanet(hn, dn_w_in[j], dn_conv_w[j], dn_a_log[j], dn_dt_bias[j],
                                 dn_out_norm_g[j], dn_w_out[j])
        else:
            mix = moba_layer(hn, mb_w_in[j], mb_w_out[j])
        h = h + mix.astype(h.dtype)
        h = h + squared_relu_mlp(rmsnorm_2(h, mlp_norm_g[i]), mlp_w_up[i], mlp_w_down[i])
    return rmsnorm_2(h, final_norm_g)


def setup_inputs(seed=0):
    out = dict(first_inputs(seed))
    for name, value in second_inputs(seed + 1).items():
        if name != "x":
            out[name + "_2"] = value
    return out


def reference(
    x, norm_mix_g, w_in, b_merge, rel_table, w_attn_out, conv_w, conv_b, w_rg_r, b_rg_r, w_rg_i,
    b_rg_i, rg_lambda, w_rnn_out, w_o, norm_ffn_g, w_ffn_in, w_ffn_out, final_norm_g,
    mix_norm_g_2, mlp_norm_g_2, dn_w_in_2, dn_conv_w_2, dn_a_log_2, dn_dt_bias_2,
    dn_out_norm_g_2, dn_w_out_2, mb_w_in_2, mb_w_out_2, mlp_w_up_2, mlp_w_down_2,
    final_norm_g_2,
):
    x = first_block(
        x, norm_mix_g, w_in, b_merge, rel_table, w_attn_out, conv_w, conv_b, w_rg_r, b_rg_r,
        w_rg_i, b_rg_i, rg_lambda, w_rnn_out, w_o, norm_ffn_g, w_ffn_in, w_ffn_out,
        final_norm_g,
    )
    return second_block(
        x, mix_norm_g_2, mlp_norm_g_2, dn_w_in_2, dn_conv_w_2, dn_a_log_2, dn_dt_bias_2,
        dn_out_norm_g_2, dn_w_out_2, mb_w_in_2, mb_w_out_2, mlp_w_up_2, mlp_w_down_2,
        final_norm_g_2,
    )


_drawn_inputs = setup_inputs


def setup_inputs(seed=0):
    import zlib

    import numpy as np

    out = dict(_drawn_inputs(seed))
    spreads = {}
    factors = {'b_merge': 32.961,
     'conv_b': 2.708,
     'b_rg_r': 59.542,
     'b_rg_i': 39.567,
     'mix_norm_g_2': 2.701,
     'dn_out_norm_g_2': 5.394,
     'final_norm_g_2': 7.711,
     'mlp_norm_g_2': 8.0}
    for name, (base, spread) in spreads.items():
        noise = np.random.default_rng([zlib.crc32(name.encode()), seed]).standard_normal(out[name].shape)
        drawn = base * np.exp(spread * noise) if base else spread * noise
        out[name] = __import__('jax').numpy.asarray(drawn.astype(out[name].dtype))
    for name, factor in factors.items():
        out[name] = (out[name] * factor).astype(out[name].dtype)
    return out
```

```python
from contextlib import ExitStack

import concourse.bass as bass
from concourse import mybir

F32 = mybir.dt.float32
F32R = mybir.dt.float32r
ALU = mybir.AluOpType
ACT = mybir.ActivationFunctionType
AX_X = mybir.AxisListType.X

P = 128
D = 1024
TOK = 256
KB = D // P
TT = TOK // P
SLOTS = 3
CW = 2048
NCOL = CW // KB
KROWS = CW // D
FF1 = 2816
FF2 = 4096
NEG = -1.0e30
EPS = 1e-6

SEGMENTS = [
    ("qk", 8), ("v", 4), ("xg", 8), ("gab", 8), ("ao", 4), ("ro", 4), ("wo", 4),
    ("fi", FF1 // P), ("fo", FF1 // P // KROWS),
    ("dq", 12), ("dz", 4), ("do", 4), ("u0", 16), ("w0", 16),
    ("mv", 4), ("mq", 8), ("mo", 4), ("u1", 16), ("w1", 16),
]
TOTAL = sum(n for _, n in SEGMENTS)

VECTORS = [
    ("norm_mix_g", 8), ("b_merge", 16), ("conv_w", 32), ("conv_b", 8), ("b_rg_r", 8),
    ("b_rg_i", 8), ("rg_lambda", 8), ("norm_ffn_g", 8), ("final_norm_g", 8),
    ("mix_norm_g_2", 16), ("mlp_norm_g_2", 16), ("dn_conv_w_2", 96), ("dn_out_norm_g_2", 1),
    ("final_norm_g_2", 8),
]
NVEC = sum(n for _, n in VECTORS)


class Segment:
    def __init__(self, name, first, n):
        self.name, self.first, self.n = name, first, n


def plan():
    out, at = {}, 0
    for name, n in SEGMENTS:
        out[name] = Segment(name, at, n)
        at += n
    return out


class Step:

    def __init__(self, seg, j, i):
        self.seg, self.j, self.i = seg, j, i
        self.base = seg.first + j
        self.slot = self.base % SLOTS

    def _plus(self, n, per):
        return n if self.i is None else self.i * per + n

    @property
    def rel(self):
        return self._plus(self.j, SLOTS)

    def rel_at(self, off):
        return self._plus(self.j + off, SLOTS)

    def count(self, off=0):
        return self._plus(self.base + 1 + off, SLOTS)

    def local(self, off=0, per=1):
        return self._plus((self.j + 1) * per + off, SLOTS * per)

    def uses(self, ahead=0, per=1):
        return self._plus(((self.base + ahead) // SLOTS + 1) * per, per)


def steps(eng, seg, body, head=0, tail=0):
    for j in range(head):
        body(Step(seg, j, None))
    turns = (seg.n - head - tail) // SLOTS
    at = head
    if turns >= 2:
        with eng.Fori(0, turns, 1) as i:
            for j in range(SLOTS):
                body(Step(seg, head + j, i))
        at += turns * SLOTS
    for j in range(at, seg.n):
        body(Step(seg, j, None))


class Chain:

    def __init__(self, sem):
        self.sem, self.n = sem, 0

    def __call__(self, ins):
        self.n += 1
        ins.then_inc(self.sem, 1)
        return self.n

    def wait(self, eng, n=None):
        eng.wait_ge(self.sem, self.n if n is None else n)


def build(nc, a):
    seg = plan()
    K1 = 1024
    base = -(-nc.sbuf_base // 64) * 64

    def sb(name, shape, dt, kib):
        return nc.alloc_sbuf_tensor_at(name, shape, dt, offset=base + int(kib * K1) // 64 * 64)

    Z = 111.5
    RAW = sb("RAW", [P, SLOTS, CW], F32, 0)
    WH = sb("WH", [P, SLOTS, CW], F32R, 24)
    WL = sb("WL", [P, SLOTS, CW], F32R, 48)
    H = sb("H", [P, KB, TOK], F32, 72)
    XH = sb("XH", [P, KB, TOK], F32R, 80)
    XL = sb("XL", [P, KB, TOK], F32R, 88)
    XN = sb("XN", [P, KB, TOK], F32, 96)
    VEC = sb("VEC", [P, NVEC], F32, 104)
    IDENT = sb("IDENT", [P, P], F32, 105)
    FLIP = sb("FLIP", [P, P], F32, Z + 88.25)
    ONES = sb("ONES", [P, P], F32, 105.5)
    NALI = sb("NALI", [P, TOK], F32, 106)
    SD = sb("SD", [P, TOK], F32, 107)
    RSTD = sb("RSTD", [P, TOK], F32, 108)
    WBA = sb("WBA", [P, KB, 16], F32, 109)
    EPSC = sb("EPSC", [P, 1], F32, 109.5)
    SP8 = sb("SP8", [P, 8], F32, 109.6)
    NSP8 = sb("NSP8", [P, 8], F32, 109.7)
    NMX = sb("NMX", [P, 4], F32, 109.8)
    SUM = sb("SUM", [P, 4], F32, 109.9)
    RSUM = sb("RSUM", [P, 4], F32, 110)
    AROW = sb("AROW", [P, 8], F32, 110.1)
    DTB = sb("DTB", [P, 8], F32, 110.2)
    SMALL = sb("SMALL", [P, 6, 16], F32, 110.3)
    GT = sb("GT", [P, 16], F32, 110.7)
    GC = sb("GC", [P, 16], F32, 110.8)
    EGC = sb("EGC", [P, 16], F32, 110.9)
    BETA = sb("BETA", [P, 16], F32, 111)
    BEG = sb("BEG", [P, 8], F32, 111.1)
    LAST = sb("LAST", [P, 8], F32, 111.2)
    QK = sb("QK", [P, 16, TOK], F32, Z + 0)
    VT = sb("VT", [P, TT, D], F32, Z + 16)
    BIAS = sb("BIAS", [P, 16, TOK], F32, Z + 24)
    BREV = sb("BREV", [P, 16, TOK], F32, Z + 40)
    OH = sb("OH", [P, KB, TOK], F32R, Z + 40)
    OL = sb("OL", [P, KB, TOK], F32R, Z + 48)
    XR = sb("XR", [P, KB, TOK + 3], F32, Z + 56)
    GR = sb("GR", [P, KB, TOK], F32, Z + 64.25)
    WRI = sb("WRI", [P, 2, KB, P], F32, Z + 72.25)
    PR = sb("PR", [P, 2, 384], F32, Z + 80.25)
    PT = sb("PT", [P, 2, 384], F32, Z + 83.25)
    EXT = sb("EXT", [16, 384], F32, Z + 86.25)
    GAB = sb("GAB", [P, 16, TOK], F32, Z + 0)
    RR = sb("RR", [P, KB, TOK], F32, Z + 24)
    RI = sb("RI", [P, KB, TOK], F32, Z + 32)
    TH = sb("TH", [P, KB, TOK], F32, Z + 56)
    MIX = sb("MIX", [P, KB, TOK], F32, Z + 16)
    MU = sb("MU", [P, KB, TOK], F32, Z + 80.25)
    HH = sb("HH", [P, 32, TOK], F32R, Z + 0)
    HL = sb("HL", [P, 32, TOK], F32R, Z + 32)
    SG = sb("SG", [P, SLOTS, 512], F32, Z + 64)
    HP = sb("HP", [P, SLOTS, 512], F32, Z + 70)
    UQ = sb("UQ", [P, 24, TOK + 3], F32, Z + 0)
    QKV = sb("QKV", [P, 24, TOK], F32, Z + 24.5)
    ZS = sb("ZS", [P, KB, TOK], F32, Z + 48.5)
    AM = sb("AM", [P, 16, P], F32, Z + 56.5)
    CM = sb("CM", [P, 16, P], F32, Z + 64.5)
    AT = sb("AT", [P, 16, P], F32, Z + 72.5)
    D1 = sb("D1", [P, 4, P], F32, Z + 80.5)
    D2 = sb("D2", [P, 4, P], F32, Z + 82.5)
    TRI = sb("TRI", [P, P], F32, Z + 84.5)
    NEGL = sb("NEGL", [P, P], F32, Z + 85)
    NEGU = sb("NEGU", [P, P], F32, Z + 85.5)
    LM = sb("LM", [P, 7, P], F32, Z + 86)
    RN = sb("RN", [P, 16, TOK], F32, Z + 0)
    SQK = sb("SQK", [P, KB, TOK], F32, Z + 16)
    D1G = sb("D1G", [P, 16, P], F32, Z + 0)
    D2G = sb("D2G", [P, 16, P], F32, Z + 8)
    TX = sb("TX", [P, 16, P], F32, Z + 0)
    TY = sb("TY", [P, 16, P], F32, Z + 8)
    P1 = sb("P1", [P, 16, P], F32, Z + 16)
    VB = sb("VB", [P, 16, P], F32, 96)
    KD = sb("KD", [P, 8, P], F32, Z + 40.5)
    KBT = sb("KBT", [P, 8, P], F32, Z + 44.5)
    VN = sb("VN", [P, 16, P], F32, Z + 0)
    ST = sb("ST", [P, 8, P], F32, Z + 64.5)
    NW = sb("NW", [P, 8, P], F32, Z + 68.5)
    OD = sb("OD", [P, KB, TOK], F32, Z + 16)
    OSQ = sb("OSQ", [P, KB, TOK], F32, Z + 56.5)

    ext_dram = nc.dram_tensor("bias_rows", [16, 384], F32, kind="Internal").ap()

    vec_at, at = {}, 0
    for name, n in VECTORS:
        vec_at[name] = at
        at += n

    def vec(name, j):
        return VEC[:, bass.ds(j + vec_at[name], 1)]

    with ExitStack() as ctx:
        PS = ctx.enter_context(nc.psum_tensor("PS", [P, 8, 512], F32))

        def sem(name):
            return ctx.enter_context(nc.semaphore(name))

        raw_in = [sem(f"raw_in{s}") for s in range(SLOTS)]
        hi_done = sem("hi_done")
        lo_done = sem("lo_done")
        mm_done = sem("mm_done")
        freed = [sem(f"freed{s}") for s in range(SLOTS)]
        names = """x_in vec_in wri_in gl2 kq_done tr_done on2 tab_in ext_ready ext_out bias_in wba_in row_in out_done
          const wri_zero flip_ready bias_masked bias_turned bias_ready sq_done sum_done sd_done xn_ready xh_ready xl_ready h4 hg xout
          scored shifted exped scaled turned pt_ready pv_done oh_done ol_done
          conv_done rg_done gates_done th_done ix_done ea_done mu_ready rt_done gl_done hs_ready
          yh_done y_done mix_ready mh_done ml_done
          dve act pool
          sg_done hp_done hh_done hl_done
          tap0 tapped silu_done dnc ba_done beta_done ey_done g_ready gc_sum gc_done
          l2sq l2sum l2sd l2done tg_done b_done dt_ready d_done gk_done at_done vt_done vt_out
          c_done p1_done p1_out q_done y1_out x1_out x_out y_out sm_ready
          vn0 vn0_out s_done s_out w_done w_out qd_done vn1 vn1_out o_done o_out osq
          osum osd on yy oo""".split()
        s = {n: sem(n) for n in names}
        s_ = type("Sems", (), s)
        block = ctx.enter_context(nc.Block())

        def cols(w, c0, n=NCOL):
            return w.rearrange("(k p) n -> p k n", p=P)[:, :, bass.ds(c0, n)]

        def rows(w, r0):
            return w.rearrange("(k p) n -> p k n", p=P)[:, bass.ds(r0, KROWS), :]

        def source(name, rel):
            if name in ("qk", "v", "xg", "gab"):
                first = {"qk": 0, "v": 2048, "xg": 3072, "gab": 5120}[name]
                return cols(a["w_in"], rel * NCOL + first)
            if name == "dq" or name == "dz":
                return cols(a["dn_w_in"], rel * NCOL + (3072 if name == "dz" else 0))
            if name == "mv":
                return cols(a["mb_w_in"], rel * NCOL + 2048)
            if name == "mq":
                return cols(a["mb_w_in"], (rel % 2) * D + (rel // 2) * NCOL)
            if name in ("u0", "u1"):
                return cols(a["mlp_w_up"][int(name[1])], rel * NCOL)
            if name in ("w0", "w1"):
                return rows(a["mlp_w_down"][int(name[1])], rel * KROWS)
            if name == "fo":
                return rows(a["w_ffn_out"], rel * KROWS)
            w = {"fi": "w_ffn_in_pairs", "ao": "w_attn_out", "ro": "w_rnn_out", "wo": "w_o", "do": "dn_w_out", "mo": "mb_w_out"}
            return cols(a[w[name]], rel * NCOL)

        def fetch(eng, st):
            if st.i is not None or st.base >= SLOTS:
                eng.wait_ge(lo_done, st.count(-SLOTS))
            name = st.seg.name
            k = KROWS if name in ("fo", "w0", "w1") else KB
            dst = RAW[:, st.slot, :].rearrange("p (k n) -> p k n", k=k)
            eng.dma_start(dst, source(name, st.rel)).then_inc(raw_in[st.slot], 16)

        def slot_of(st, ahead):
            return (st.base + ahead) % SLOTS

        def ahead_of(st):
            return None if st.i is None and st.base + SLOTS - 1 >= TOTAL else SLOTS - 1

        def split_hi(act, st, ahead="next"):
            n = ahead_of(st) if ahead == "next" else ahead
            if n is None:
                return
            k = slot_of(st, n)
            act.wait_ge(raw_in[k], st.uses(n, 16))
            if st.i is not None or st.base + n >= SLOTS:
                act.wait_ge(mm_done, st.count(n - SLOTS))
            act.activation(WH[:, k], RAW[:, k], ACT.Copy).then_inc(hi_done, 1)

        def split_lo(dve, st, ahead="next"):
            n = ahead_of(st) if ahead == "next" else ahead
            if n is None:
                return
            k = slot_of(st, n)
            dve.wait_ge(hi_done, st.count(n))
            dve.tensor_tensor(WL[:, k], RAW[:, k], WH[:, k].bitcast(F32), ALU.subtract).then_inc(lo_done, 1)

        def product(pe, out, wh, wl, xh, xl, start, stop):
            pe.matmul(out, wh, xh, start=start, stop=False, skip_group_check=True)
            pe.matmul(out, wh, xl, start=False, stop=False, skip_group_check=True)
            return pe.matmul(out, wl, xh, start=False, stop=stop, skip_group_check=True)

        def bank_free(pe, st):
            if st.i is not None or st.base >= SLOTS:
                pe.wait_ge(freed[st.slot], st.uses(-SLOTS))

        def multiply(pe, st, xh, xl, pieces=None, tokens_out=False):
            pe.wait_ge(lo_done, st.count())
            bank_free(pe, st)
            h = WH[:, st.slot].rearrange("p (k n) -> p k n", k=KB)
            l = WL[:, st.slot].rearrange("p (k n) -> p k n", k=KB)
            for b in range(2):
                out = PS[:, st.slot, b * TOK:(b + 1) * TOK]
                part = slice(b * P, b * P + P)
                for k in range(KB):
                    if pieces is not None and b == 0 and k % 2 == 0:
                        pe.wait_ge(pieces[0], pieces[1] + k // 2 + 1)
                    if tokens_out:
                        mm = product_t(pe, out, xh[:, k, part], xl[:, k, part], h[:, k], l[:, k], k == 0, k == KB - 1)
                    else:
                        mm = product(pe, out, h[:, k, part], l[:, k, part], xh[:, k], xl[:, k], k == 0, k == KB - 1)
            mm.then_inc(mm_done, 1)

        def product_t(pe, out, xh, xl, wh, wl, start, stop):
            pe.matmul(out, xh, wh, start=start, stop=False, skip_group_check=True)
            pe.matmul(out, xh, wl, start=False, stop=False, skip_group_check=True)
            return pe.matmul(out, xl, wh, start=False, stop=stop, skip_group_check=True)

        def multiply_rows(pe, st, ready):
            pe.wait_ge(lo_done, st.count())
            pe.wait_ge(s_.hl_done, ready)
            h = WH[:, st.slot].rearrange("p (k n) -> p k n", k=KROWS)
            l = WL[:, st.slot].rearrange("p (k n) -> p k n", k=KROWS)
            first = st.i is None and st.j == 0
            last = st.i is None and st.j == st.seg.n - 1
            for k in range(KROWS):
                xh = HH[:, bass.ds(st.rel * KROWS + k, 1), :].rearrange("p k t -> p (k t)")
                xl = HL[:, bass.ds(st.rel * KROWS + k, 1), :].rearrange("p k t -> p (k t)")
                for b in range(KB):
                    mm = product(pe, PS[:, b // 2, (b % 2) * TOK:(b % 2 + 1) * TOK],
                                 h[:, k, b * P:(b + 1) * P], l[:, k, b * P:(b + 1) * P], xh, xl,
                                 first and k == 0 and b % 2 == 0, last and k == KROWS - 1)
            mm.then_inc(mm_done, 1)

        def uses_upto(sg, k):
            return sum(1 for c in range(sg.first + sg.n) if c % SLOTS == k)

        def banks_free(pe, sg):
            for k in range(SLOTS):
                pe.wait_ge(freed[k], uses_upto(sg, k) - sum(1 for c in range(sg.first, sg.first + sg.n) if c % SLOTS == k))

        def add_rows(dve, sg, nth):
            dve.wait_ge(mm_done, sg.first + sg.n)
            for b in range(4):
                hb = H[:, 2 * b:2 * b + 2, :]
                ins = dve.tensor_tensor(hb, hb, PS[:, b, :].rearrange("p (c t) -> p c t", c=2), ALU.add)
                if b < SLOTS:
                    ins.then_inc(freed[b], sum(1 for c in range(sg.first, sg.first + sg.n) if c % SLOTS == b))
                else:
                    ins.then_inc(s_.h4, 1)

        NORMS = [
            (None, "norm_mix_g", 0, "split"), ("wo", "norm_ffn_g", 0, "split"),
            ("fo", "final_norm_g", 0, "h"), ("hg", "mix_norm_g_2", 0, "split"),
            ("do", "mlp_norm_g_2", 0, "split"), ("w0", "mix_norm_g_2", 8, "split"),
            ("mo", "mlp_norm_g_2", 8, "split"), ("w1", "final_norm_g_2", 0, "out"),
        ]
        split_no = {m: sum(x[3] == "split" for x in NORMS[:m]) for m in range(len(NORMS))}
        h4_no = {"fo": 1, "w0": 2, "w1": 3}

        def wait_h(eng, m, p):
            src = NORMS[m][0]
            if src is None:
                if p == 0:
                    eng.wait_ge(s_.x_in, 16)
            elif src == "hg":
                eng.wait_ge(s_.hg, p + 1)
            elif src in h4_no:
                if p < SLOTS:
                    eng.wait_ge(freed[p], uses_upto(seg[src], p))
                else:
                    eng.wait_ge(s_.h4, h4_no[src])
            else:
                c = seg[src].first + p
                eng.wait_ge(freed[c % SLOTS], c // SLOTS + 1)

        def norm_act(act, m):
            for p in range(4):
                wait_h(act, m, p)
                act.activation(XN[:, 2 * p:2 * p + 2], H[:, 2 * p:2 * p + 2], ACT.Square).then_inc(s_.sq_done, 1)
            act.wait_ge(s_.sum_done, m + 1)
            act.activation(SD[:], PS[:, 4, 0:TOK], ACT.Sqrt, bias=EPSC[:], scale=1.0 / D).then_inc(s_.sd_done, 1)
            if NORMS[m][3] == "split":
                for p in range(4):
                    act.wait_ge(s_.xn_ready, 4 * split_no[m] + p + 1)
                    act.activation(XH[:, 2 * p:2 * p + 2], XN[:, 2 * p:2 * p + 2], ACT.Copy).then_inc(s_.xh_ready, 1)

        def norm_pe(pe, m):
            for p in range(4):
                pe.wait_ge(s_.sq_done, 4 * m + p + 1)
                for j in (2 * p, 2 * p + 1):
                    mm = pe.matmul(PS[:, 4, 0:TOK], ONES[:], XN[:, j], start=(j == 0), stop=(j == KB - 1))
            mm.then_inc(s_.sum_done, 1)

        def norm_dve(dve, ch, m):
            _, name, c0, kind = NORMS[m]
            dve.wait_ge(s_.sd_done, m + 1)
            n = ch(dve.reciprocal(RSTD[:], SD[:]))
            ch.wait(dve, n)
            out, done = {"split": (XN, s_.xn_ready), "h": (H, s_.hg), "out": (XN, s_.xout)}[kind]

            def low(p):
                dve.wait_ge(s_.xh_ready, 4 * split_no[m] + p + 1)
                dve.tensor_tensor(XL[:, 2 * p:2 * p + 2], XN[:, 2 * p:2 * p + 2],
                                  XH[:, 2 * p:2 * p + 2].bitcast(F32), ALU.subtract).then_inc(s_.xl_ready, 1)

            for p in range(4):
                for j in (2 * p, 2 * p + 1):
                    ins = dve.scalar_tensor_tensor(out=out[:, j], in0=H[:, j], scalar=vec(name, c0 + j),
                                                   in1=RSTD[:], op0=ALU.mult, op1=ALU.mult)
                ins.then_inc(done, 1)
                if kind == "split" and p:
                    low(p - 1)
            if kind == "split":
                low(3)

        SCALE = {False: 64.0 ** -0.5, True: 128.0 ** -0.5}

        def heads(n):
            for e in range(2):
                if n < 8:
                    rows_, j = slice(64 * e, 64 * e + 64), n
                    yield 2 * n + e, QK[rows_, j], QK[rows_, 8 + j], slice((2 * n + e) * 64, (2 * n + e) * 64 + 64), PS[rows_, 7, 0:TOK]
                else:
                    h = 2 * (n - 8) + e
                    yield h, QK[:, h], QK[:, 8 + h], slice(h * P, h * P + P), PS[:, 7, e * TOK:(e + 1) * TOK]

        def attn_scores(pe, n):
            for e, (_, q, k, _, _) in enumerate(heads(n)):
                pe.matmul(PS[:, 3 + e, 0:P], q[:, 0:P], k[:, 0:P], start=True, stop=True)
                mm = pe.matmul(PS[:, 3 + e, P:384], q[:, P:TOK], k[:, 0:TOK], start=True, stop=True)
            mm.then_inc(s_.scored, 1)

        def attn_shift(dve, ch, n):
            moba = n >= 8
            dve.wait_ge(s_.scored, n + 1)
            for e, (h, *_) in enumerate(heads(n)):
                for t, w in ((0, P), (1, TOK)):
                    cols_ = slice(P * t, P * t + w)
                    if moba:
                        bias, out = NALI[:, TOK - w:TOK], dict(in0=NALI[:, TOK - w:TOK], in1=PS[:, 3 + e, cols_])
                        k = 2.0 ** -(h + 1) / SCALE[True]
                    else:
                        out = dict(in0=PS[:, 3 + e, cols_], in1=BIAS[:, h, TOK - w:TOK])
                        k = SCALE[False]
                    ch(dve.scalar_tensor_tensor(out=PR[:, e, cols_], scalar=k, op0=ALU.mult, op1=ALU.add, **out))
            for e in range(2):
                for t, w in ((0, P), (1, TOK)):
                    ch.wait(dve, ch.n - 3)
                    ch(dve.tensor_reduce(out=NMX[:, 2 * e + t:2 * e + t + 1], in_=PR[:, e, P * t:P * t + w],
                                         axis=AX_X, op=ALU.max))
            ch.wait(dve)
            dve.tensor_scalar(NMX[:], NMX[:], -SCALE[True] if moba else -1.0, None, ALU.mult).then_inc(s_.shifted, 1)

        def attn_exp(act, n):
            act.wait_ge(s_.shifted, n + 1)
            for e in range(2):
                for t, w in ((0, P), (1, TOK)):
                    i = 2 * e + t
                    pr = PR[:, e, P * t:P * t + w]
                    act.activation(pr, pr, ACT.Exp, bias=NMX[:, i:i + 1], scale=SCALE[True] if n >= 8 else 1.0,
                                   accum_out=SUM[:, i:i + 1]).then_inc(s_.exped, 1)

        def attn_scale(dve, ch, n):
            dve.wait_ge(s_.exped, 4 * n + 4)
            ch(dve.reciprocal(RSUM[:], SUM[:]))
            ch.wait(dve)
            for e in range(2):
                for t, w in ((0, P), (1, TOK)):
                    pr = PR[:, e, P * t:P * t + w]
                    dve.tensor_scalar(pr, pr, RSUM[:, 2 * e + t:2 * e + t + 1], None, ALU.mult).then_inc(s_.scaled, 1)

        def attn_turn(pe, n):
            pe.wait_ge(s_.scaled, 4 * n + 4)
            if n:
                pe.wait_ge(s_.pt_ready, 2 * n)
            for e in range(2):
                for b in range(3):
                    mm = pe.transpose(PS[:, 5 + e, P * b:P * b + P], PR[:, e, P * b:P * b + P], IDENT[:])
            mm.then_inc(s_.turned, 1)

        def attn_pt(act, n):
            act.wait_ge(s_.turned, n + 1)
            for e in range(2):
                act.activation(PT[:, e], PS[:, 5 + e, 0:384], ACT.Copy).then_inc(s_.pt_ready, 1)

        def attn_pv(pe, n):
            pe.wait_ge(s_.pt_ready, 2 * n + 2)
            if n:
                pe.wait_ge(s_.ol_done, n)
            for e, (_, _, _, vc, out) in enumerate(heads(n)):
                pe.matmul(out[:, 0:P], VT[:, 0, vc], PT[:, e, 0:P], start=True, stop=True, skip_group_check=True)
                pe.matmul(out[:, P:TOK], VT[:, 0, vc], PT[:, e, P:TOK], start=True, stop=False, skip_group_check=True)
                mm = pe.matmul(out[:, P:TOK], VT[:, 1, vc], PT[:, e, TOK:384], start=False, stop=True, skip_group_check=True)
            mm.then_inc(s_.pv_done, 1)

        def out_blocks(n):
            if n < 8:
                return slice(n, n + 1), PS[:, 7, 0:TOK].rearrange("p (c t) -> p c t", c=1)
            return slice(2 * (n - 8), 2 * (n - 8) + 2), PS[:, 7, :].rearrange("p (c t) -> p c t", c=2)

        def attn_oh(act, n):
            act.wait_ge(s_.pv_done, n + 1)
            b, ps = out_blocks(n)
            act.activation(OH[:, b], ps, ACT.Copy).then_inc(s_.oh_done, 1)

        def attn_ol(dve, n):
            dve.wait_ge(s_.oh_done, n + 1)
            b, ps = out_blocks(n)
            dve.tensor_tensor(OL[:, b], ps, OH[:, b].bitcast(F32), ALU.subtract).then_inc(s_.ol_done, 1)

        def two(ap):
            return ap.rearrange("p (c t) -> p c t", c=2)

        def bank(st):
            return two(PS[:, st.slot, :])

        @block.sync
        def _(sp):
            for name, n in SEGMENTS:
                steps(sp, seg[name], lambda st: fetch(sp, st), head=SLOTS if name == "qk" else 0)
            for p in range(4):
                sp.wait_ge(s_.xout, p + 1)
                sp.dma_start(a["out"].rearrange("(j p) t -> p j t", p=P)[:, 2 * p:2 * p + 2], XN[:, 2 * p:2 * p + 2]).then_inc(s_.out_done, 16)
            sp.wait_ge(s_.out_done, 64)

        @block.gpsimd
        def _(pool):
            pc = Chain(s_.pool)
            pc(pool.memset(ONES[:], 1.0))
            pool.memset(EPSC[:], EPS).then_inc(s_.const, 1)
            pc(pool.memset(WRI[:], 0.0))
            pool.memset(XR[:, :, 0:3], 0.0).then_inc(s_.wri_zero, 1)
            pc(pool.memset(IDENT[:], 0.0))
            pc(pool.memset(FLIP[:], 0.0))
            pc.wait(pool)
            pool.affine_select(out=IDENT[:], in_=IDENT[:], compare_op=ALU.not_equal, fill=1.0, base=0,
                               pattern=[[-1, P]], channel_multiplier=1).then_inc(s_.const, 1)
            pool.affine_select(out=FLIP[:], in_=FLIP[:], compare_op=ALU.not_equal, fill=1.0, base=1 - P,
                               pattern=[[1, P]], channel_multiplier=1).then_inc(s_.flip_ready, 1)
            pool.wait_ge(s_.tab_in, 16)
            pool.tensor_copy(EXT[:, 0:127], EXT[:, 127:128].to_broadcast([16, 127])).then_inc(s_.ext_ready, 1)
            iot = nc.alloc_sbuf_tensor_at("IOT", [P, TOK], mybir.dt.int32, offset=base + int((Z + 89) * K1))
            pc(pool.iota(iot[:], pattern=[[1, TOK]], base=-P, channel_multiplier=-1))
            pc.wait(pool)
            pc(pool.tensor_copy(NALI[:], iot[:]))
            pc.wait(pool)
            pool.affine_select(out=NALI[:], in_=NALI[:], compare_op=ALU.is_ge, fill=NEG, base=P,
                               pattern=[[-1, TOK]], channel_multiplier=1).then_inc(s_.const, 1)
            pool.wait_ge(s_.bias_in, 16)
            pool.wait_ge(s_.const, 3)
            pool.memset(BREV[64:P, :, 192:TOK], NEG).then_inc(s_.bias_masked, 1)

            pool.wait_ge(s_.hg, 4)
            pc(pool.memset(UQ[:, :, 0:3], 0.0))
            pc(pool.memset(TRI[:], 1.0))
            pc(pool.memset(NEGL[:], 0.0))
            pc(pool.memset(NEGU[:], 0.0))
            pc(pool.memset(LM[:], 1.0))
            pc.wait(pool)
            pc(pool.affine_select(out=TRI[:], in_=TRI[:], compare_op=ALU.is_ge, fill=0.0, base=0,
                                  pattern=[[1, P]], channel_multiplier=-1))
            pc(pool.affine_select(out=NEGL[:], in_=NEGL[:], compare_op=ALU.is_gt, fill=NEG, base=0,
                                  pattern=[[-1, P]], channel_multiplier=1))
            pc(pool.affine_select(out=NEGU[:], in_=NEGU[:], compare_op=ALU.is_ge, fill=NEG, base=0,
                                  pattern=[[1, P]], channel_multiplier=-1))
            for l in range(7):
                w = 1 << l
                m = LM[:, l].rearrange("p (b two c) -> p b two c", two=2, c=w)
                pc(pool.memset(m[:, :, 1, :], 0.0))
                pc.wait(pool)
                pc(pool.affine_select(out=m[:, :, 0, :], in_=m[:, :, 0, :], compare_op=ALU.is_ge, fill=0.0, base=-w,
                                      pattern=[[-2 * w, P // (2 * w)], [0, w]], channel_multiplier=1))
                pc.wait(pool)
                pc(pool.affine_select(out=m[:, :, 0, :], in_=m[:, :, 0, :], compare_op=ALU.is_ge, fill=0.0, base=2 * w - 1,
                                      pattern=[[2 * w, P // (2 * w)], [0, w]], channel_multiplier=-1))
            pc.wait(pool)
            pool.memset(D1[:, 0, 0:1], 0.0).then_inc(s_.on, 1)

            pool.wait_ge(s_.g_ready, 1)
            pool.wait_ge(s_.l2done, 8)
            for n in range(16):
                pool.tensor_scalar(CM[:, n], TRI[:], GT[:, n:n + 1], 1.0, ALU.mult, ALU.mult).then_inc(s_.tg_done, 1)
            pool.wait_ge(s_.at_done, 4)
            for l in range(7):
                for g in range(4):
                    n = 4 * l + g
                    if l == 1:
                        pool.wait_ge(s_.y_out, 2 * g + 2)
                    elif l > 1:
                        pool.wait_ge(s_.p1_done, n - 7)
                    pool.tensor_tensor(CM[:, 4 * g:4 * g + 4], AM[:, 4 * g:4 * g + 4],
                                       LM[:, l, None, :].to_broadcast([P, 4, P]), ALU.mult).then_inc(s_.c_done, 1)

        def hidden_hi(act, st, width):
            k = slot_of(st, -1)
            act.activation(hid(HH, st, width), HP[:, k, 0:width * TOK].rearrange("p (c t) -> p c t", c=width),
                           ACT.Copy).then_inc(s_.hh_done, 1)

        def hid(t, st, width):
            return t[:, bass.ds(st.rel_at(-1) * width, width), :]

        def hidden_lo(dve, st, width, base_):
            k = slot_of(st, -1)
            dve.wait_ge(s_.hh_done, st.local(base_ - 1))
            dve.tensor_tensor(hid(HL, st, width), HP[:, k, 0:width * TOK].rearrange("p (c t) -> p c t", c=width),
                              hid(HH, st, width).bitcast(F32), ALU.subtract).then_inc(s_.hl_done, 1)

        HBASE = {"fi": 0, "u0": 22, "u1": 38}

        def silu_ready(act, st):
            act.wait_ge(freed[slot_of(st, -1)], st.uses(-1))

        def square_ready(b0):
            def ready(act, st):
                act.wait_ge(s_.hp_done, st.local(b0 - 1))
            return ready

        @block.scalar
        def _(act):
            act.dma_start(H[:], a["x"].rearrange("(j p) t -> p j t", p=P)).then_inc(s_.x_in, 16)
            act.dma_start(VEC[:], a["vectors"]).then_inc(s_.vec_in, 16)
            act.dma_start(EXT[:, 127:384], a["rel_reversed"]).then_inc(s_.tab_in, 16)
            act.dma_start(AROW[:], a["dn_a_log"].partition_broadcast(P)).then_inc(s_.row_in, 16)
            act.dma_start(DTB[:], a["dn_dt_bias"].partition_broadcast(P)).then_inc(s_.row_in, 16)
            act.dma_start(WBA[:], cols(a["dn_w_in"], 4096, 16)).then_inc(s_.row_in, 16)
            act.wait_ge(s_.wri_zero, 1)
            act.wait_ge(s_.pool, 2)
            for r, w in enumerate(("w_rg_r", "w_rg_i")):
                for e in range(2):
                    act.dma_start(WRI[64 * e:64 * e + 64, r, :, 64 * e:64 * e + 64],
                                  a[w].rearrange("(j e) d f -> e d j f", e=2)[e]).then_inc(s_.wri_in, 16)
            act.wait_ge(s_.ext_ready, 1)
            act.dma_start(ext_dram, EXT[:]).then_inc(s_.ext_out, 16)
            act.wait_ge(s_.const, 1)
            norm_act(act, 0)
            act.wait_ge(s_.ext_out, 16)
            act.dma_start(BREV[:], bass.AP(tensor=ext_dram.tensor, offset=0, ap=[[1, P], [384, 16], [1, TOK]])).then_inc(s_.bias_in, 16)

            act.wait_ge(s_.ey_done, 1)
            act.activation(SMALL[:, 1, 0:8], SMALL[:, 1, 0:8], ACT.Exp, scale=-1.0).then_inc(s_.sm_ready, 1)

            first = Step(seg["qk"], 0, None)
            for n in range(SLOTS - 1):
                split_hi(act, first, n)
            def qk(st):
                split_hi(act, st)
                if st.i is None and st.j == 2:
                    for n in range(8):
                        act.wait_ge(s_.bias_turned, n + 1)
                        act.activation(BIAS[:, 2 * n:2 * n + 2], two(PS[:, 5 + n % 3, :]), ACT.Copy).then_inc(s_.bias_ready, 1)
            steps(act, seg["qk"], qk, head=SLOTS)
            steps(act, seg["v"], lambda st: split_hi(act, st))

            for st in (Step(seg["xg"], j, None) for j in range(8)):
                attn_exp(act, st.j)
                split_hi(act, st)
                if st.j:
                    attn_oh(act, st.j - 1)
                attn_pt(act, st.j)

            def sigmoid(out, ps, bias):
                return act.activation(out, ps, ACT.Sigmoid, bias=bias)

            def decay(j):
                act.wait_ge(s_.gates_done, 2 * j + 1)
                act.activation(RR[:, j], RR[:, j], ACT.Exp, scale=NSP8[:, j:j + 1]).then_inc(s_.ea_done, 1)

            for st in (Step(seg["gab"], j, None) for j in range(8)):
                j = st.j
                split_hi(act, st)
                if j == 0:
                    attn_oh(act, 7)
                if j == 5:
                    for b in range(4):
                        decay(b)
                act.wait_ge(s_.rg_done, j + 1)
                sigmoid(RR[:, j], PS[:, 3 + j % 2, 0:TOK], vec("b_rg_r", j)).then_inc(s_.gates_done, 1)
                sigmoid(RI[:, j], PS[:, 3 + j % 2, TOK:512], vec("b_rg_i", j)).then_inc(s_.gates_done, 1)
                act.wait_ge(mm_done, st.count())
                sigmoid(GAB[:, 2 * j], PS[:, st.slot, 0:TOK], vec("b_merge", 2 * j))
                sigmoid(GAB[:, 2 * j + 1], PS[:, st.slot, TOK:512], vec("b_merge", 2 * j + 1)).then_inc(freed[st.slot], 1)
                act.wait_ge(s_.gates_done, 2 * j + 1)
                act.activation(TH[:, j], RR[:, j], ACT.Tanh, scale=SP8[:, j:j + 1]).then_inc(s_.th_done, 1)

            for st in (Step(seg["ao"], j, None) for j in range(4)):
                split_hi(act, st)
                if st.j == 0:
                    for b in range(4, 8):
                        decay(b)
                    act.wait_ge(s_.mu_ready, 2)
                    act.activation(MU[:], MU[:], ACT.Sqrt).then_inc(s_.rt_done, 1)
                    act.activation(GR[:], GR[:], ACT.Gelu_apprx_tanh).then_inc(s_.gl_done, 1)
            for p in range(4):
                act.wait_ge(s_.hs_ready, p + 1)
                act.activation(XH[:, 2 * p:2 * p + 2], XN[:, 2 * p:2 * p + 2], ACT.Copy).then_inc(s_.yh_done, 1)
            for st in (Step(seg["ro"], j, None) for j in range(4)):
                split_hi(act, st)
                act.wait_ge(s_.mix_ready, st.j + 1)
                act.activation(OH[:, 2 * st.j:2 * st.j + 2], MIX[:, 2 * st.j:2 * st.j + 2], ACT.Copy).then_inc(s_.mh_done, 1)
            steps(act, seg["wo"], lambda st: split_hi(act, st))

            norm_act(act, 1)

            def gate(st):
                split_hi(act, st)
                act.wait_ge(mm_done, st.count())
                if st.i is not None or st.j:
                    silu_ready(act, st)
                act.activation(SG[:, st.slot, 0:TOK], PS[:, st.slot, 0:TOK], ACT.Silu).then_inc(s_.sg_done, 1)
                if st.i is not None or st.j:
                    hidden_hi(act, st, 1)
            steps(act, seg["fi"], gate, head=1)
            end = Step(seg["fi"], seg["fi"].n, None)
            silu_ready(act, end)
            hidden_hi(act, end, 1)
            steps(act, seg["fo"], lambda st: split_hi(act, st))

            norm_act(act, 2)
            norm_act(act, 3)

            def tap0(st):
                for b in range(2):
                    blk = st.rel_at(-1) * 2 + b
                    act.activation(QKV[:, bass.ds(blk, 1), :], UQ[:, bass.ds(blk, 1), 0:TOK], ACT.Copy,
                                   scale=vec("dn_conv_w_2", blk)).then_inc(s_.tap0, 1)

            def silu(st):
                blk = QKV[:, bass.ds(st.rel_at(-2) * 2, 2), :]
                act.activation(blk, blk, ACT.Silu).then_inc(s_.silu_done, 1)

            def dq(st):
                if st.i is not None or st.j >= 1:
                    act.wait_ge(freed[slot_of(st, -1)], st.uses(-1))
                if st.i is not None or st.j >= 2:
                    act.wait_ge(s_.tapped, st.local(-12, 6))
                split_hi(act, st)
                if st.i is None and st.j == 0:
                    act.wait_ge(s_.ba_done, 1)
                    act.activation(BETA[:].rearrange("p (c h) -> p c h", c=TT),
                                   PS[:, 3, 256:288].rearrange("p (c x) -> p c x", c=TT)[:, :, 0:8], ACT.Sigmoid).then_inc(s_.beta_done, 1)
                    act.wait_ge(s_.ey_done, 2)
                    act.activation(SMALL[:, 1], SMALL[:, 1], ACT.Exp, scale=-1.0).then_inc(s_.sm_ready, 1)
                    act.activation(AROW[:], AROW[:], ACT.Exp).then_inc(s_.sm_ready, 1)
                if st.i is None and st.j == 1:
                    act.wait_ge(s_.gc_done, 1)
                    act.activation(EGC[:], GC[:], ACT.Exp).then_inc(s_.sm_ready, 1)
                if st.i is not None or st.j >= 1:
                    tap0(st)
                if st.i is not None or st.j >= 2:
                    silu(st)
            steps(act, seg["dq"], dq, head=3)
            for st in (Step(seg["dz"], j, None) for j in range(4)):
                split_hi(act, st)
                q = Step(seg["dq"], seg["dq"].n + st.j, None)
                if st.j == 0:
                    act.wait_ge(freed[slot_of(q, -1)], q.uses(-1))
                    tap0(q)
                if st.j <= 1:
                    act.wait_ge(s_.tapped, q.local(-12, 6))
                    silu(q)
                act.wait_ge(mm_done, st.count())
                act.activation(ZS[:, 2 * st.j:2 * st.j + 2], bank(st), ACT.Silu).then_inc(freed[st.slot], 1)

            act.wait_ge(s_.silu_done, seg["dq"].n)
            act.activation(XN[:], QKV[:, 0:8], ACT.Square).then_inc(s_.l2sq, 1)
            act.activation(SQK[:], QKV[:, 8:16], ACT.Square).then_inc(s_.l2sq, 1)
            for u in range(8):
                act.wait_ge(s_.l2sum, u + 1)
                act.activation(RN[:, 2 * u:2 * u + 2], two(PS[:, (3 + u) % 8, :]), ACT.Sqrt, bias=EPSC[:]).then_inc(s_.l2sd, 1)
            for g in range(4):
                for t, d in enumerate((D1G, D2G)):
                    act.wait_ge(s_.dt_ready, 2 * g + t + 1)
                    act.activation(d[:, 4 * g:4 * g + 4], d[:, 4 * g:4 * g + 4], ACT.Exp).then_inc(s_.d_done, 1)
                if g >= 2:
                    if g == 3:
                        act.wait_ge(s_.qd_done, 1)
                    act.activation(D1[:], PS[:, 3 + g, :].rearrange("p (n i) -> p n i", n=4), ACT.Exp).then_inc(s_.gl2, 1)
            for n in range(24):
                g = n % 4
                act.wait_ge(s_.p1_done, n + 1)
                act.activation(P1[:, 4 * g:4 * g + 4], PS[:, n % 2, :].rearrange("p (n i) -> p n i", n=4), ACT.Copy).then_inc(s_.p1_out, 1)
            for g in range(2):
                act.wait_ge(s_.w_done, g + 1)
                act.activation(NW[:, 4 * g:4 * g + 4], PS[:, g, :].rearrange("p (n i) -> p n i", n=4), ACT.Copy, scale=-1.0).then_inc(s_.w_out, 1)
            for u in range(4):
                act.wait_ge(s_.o_out, u + 1)
                act.activation(OSQ[:, 2 * u:2 * u + 2], OD[:, 2 * u:2 * u + 2], ACT.Square).then_inc(s_.osq, 1)
            for u in range(4):
                act.wait_ge(s_.osum, u + 1)
                act.activation(RN[:, 2 * u:2 * u + 2], two(PS[:, 2 + u, :]), ACT.Sqrt, bias=EPSC[:], scale=1.0 / P).then_inc(s_.osd, 1)
            for u in range(4):
                act.wait_ge(s_.on2, u + 1)
                act.activation(XH[:, 2 * u:2 * u + 2], OD[:, 2 * u:2 * u + 2], ACT.Copy).then_inc(s_.oo, 1)
            steps(act, seg["do"], lambda st: split_hi(act, st))

            def mlp(layer):
                norm_act(act, 4 + 2 * layer)
                sq = square_ready(16 * layer)

                def up(st):
                    split_hi(act, st)
                    act.wait_ge(mm_done, st.count())
                    if st.i is not None or st.j:
                        sq(act, st)
                    act.activation(SG[:, st.slot, :], PS[:, st.slot, :], ACT.Relu).then_inc(freed[st.slot], 1)
                    if st.i is not None or st.j:
                        hidden_hi(act, st, 2)
                u = seg[f"u{layer}"]
                steps(act, u, up, head=1)
                end = Step(u, u.n, None)
                sq(act, end)
                hidden_hi(act, end, 2)
                w = seg[f"w{layer}"]
                steps(act, w, lambda st: split_hi(act, st), tail=SLOTS - 1 if layer else 0)
                norm_act(act, 5 + 2 * layer)

            mlp(0)
            steps(act, seg["mv"], lambda st: split_hi(act, st))
            for t in range(11):
                if t >= 3 and t % 2:
                    attn_exp(act, 8 + (t - 3) // 2)
                if t < 8:
                    split_hi(act, Step(seg["mq"], t, None))
                if t >= 3 and t % 2:
                    attn_pt(act, 8 + (t - 3) // 2)
                if t >= 4 and t % 2 == 0:
                    attn_oh(act, 8 + (t - 4) // 2)
            steps(act, seg["mo"], lambda st: split_hi(act, st))
            mlp(1)

        @block.vector
        def _(dve):
            ch = Chain(s_.dve)

            def softplus(y, n, ready, nth):
                v = [SMALL[:, i, 0:n] for i in range(6)]
                ch.wait(dve)
                dve.scalar_tensor_tensor(out=v[1], in0=v[0], scalar=-1.0, in1=v[0], op0=ALU.mult, op1=ALU.max).then_inc(s_.ey_done, 1)
                dve.wait_ge(s_.sm_ready, ready)
                ch(dve.tensor_scalar(v[2], v[1], 2.0, None, ALU.add))
                ch.wait(dve)
                ch(dve.reciprocal(v[2], v[2]))
                ch.wait(dve)
                ch(dve.tensor_tensor(v[2], v[2], v[1], ALU.mult))
                ch.wait(dve)
                ch(dve.tensor_tensor(v[3], v[2], v[2], ALU.mult))
                ch.wait(dve)
                ch(dve.tensor_scalar(v[4], v[3], 1.0 / 17, None, ALU.mult))
                for k in range(7, 0, -1):
                    ch.wait(dve)
                    ch(dve.scalar_tensor_tensor(out=v[4], in0=v[4], scalar=1.0 / (2 * k + 1), in1=v[3], op0=ALU.add, op1=ALU.mult))
                ch.wait(dve)
                ch(dve.scalar_tensor_tensor(out=v[4], in0=v[4], scalar=1.0, in1=v[2], op0=ALU.add, op1=ALU.mult))
                ch(dve.tensor_scalar(v[5], v[0], 0.0, None, ALU.max))
                ch.wait(dve)
                ch(dve.scalar_tensor_tensor(out=v[5], in0=v[4], scalar=2.0, in1=v[5], op0=ALU.mult, op1=ALU.add))
                ch.wait(dve)
                return v[5]

            dve.wait_ge(s_.vec_in, 16)
            norm_dve(dve, ch, 0)
            ch(dve.tensor_scalar(SMALL[:, 0, 0:8], VEC[:, vec_at["rg_lambda"]:vec_at["rg_lambda"] + 8], -1.0, None, ALU.mult))
            sp = softplus(None, 8, 1, 0)
            ch(dve.tensor_scalar(SP8[:], sp, 8.0, None, ALU.mult))
            ch(dve.tensor_scalar(NSP8[:], sp, -8.0, None, ALU.mult))

            def read_out(st, out):
                dve.wait_ge(mm_done, st.count())
                dve.tensor_copy(out, bank(st)).then_inc(freed[st.slot], 1)

            first = Step(seg["qk"], 0, None)
            for n in range(SLOTS - 1):
                split_lo(dve, first, n)

            def qk(st):
                split_lo(dve, st)
                read_out(st, QK[:, bass.ds(st.rel * 2, 2), :])
            steps(dve, seg["qk"], qk, head=SLOTS)

            def v(st):
                split_lo(dve, st)
                read_out(st, VT[:, :, bass.ds(st.rel * NCOL, NCOL)])
            steps(dve, seg["v"], v)

            def conv(c):
                for t in range(4):
                    for j in (2 * c, 2 * c + 1):
                        if t == 0:
                            if j == 2 * c:
                                dve.wait_ge(freed[(seg["xg"].first + c) % SLOTS], (seg["xg"].first + c) // SLOTS + 1)
                            ch(dve.tensor_scalar(XN[:, j], XR[:, j, 0:TOK], vec("conv_w", j), vec("conv_b", j), ALU.mult, ALU.add))
                            continue
                        ch.wait(dve, ch.n - (0 if t == 3 and j % 2 else 1))
                        ins = dve.scalar_tensor_tensor(out=XN[:, j], in0=XR[:, j, t:t + TOK], scalar=vec("conv_w", 8 * t + j),
                                                       in1=XN[:, j], op0=ALU.mult, op1=ALU.add)
                        if t < 3:
                            ch(ins)
                        else:
                            ins.then_inc(s_.conv_done, 1)

            dve.wait_ge(s_.bias_ready, 8)
            for st in (Step(seg["xg"], j, None) for j in range(8)):
                j = st.j
                attn_shift(dve, ch, j)
                split_lo(dve, st)
                attn_scale(dve, ch, j)
                read_out(st, XR[:, 2 * j:2 * j + 2, 3:TOK + 3] if j < 4 else GR[:, 2 * j - 8:2 * j - 6])
                if 1 <= j <= 4:
                    conv(j - 1)
                if j:
                    attn_ol(dve, j - 1)
            for st in (Step(seg["gab"], j, None) for j in range(8)):
                split_lo(dve, st)
                if st.j == 0:
                    attn_ol(dve, 7)
                dve.wait_ge(s_.gates_done, 2 * st.j + 2)
                ch(dve.tensor_tensor(RI[:, st.j], RI[:, st.j], XN[:, st.j], ALU.mult))

            def scan():
                dve.wait_ge(s_.rt_done, 1)
                ch(dve.tensor_tensor(RI[:], RI[:], MU[:], ALU.mult))
                ch.wait(dve)
                for b in range(KB):
                    ch(dve.tensor_tensor_scan(XN[:, b], RR[:, b], RI[:, b], 0.0, ALU.mult, ALU.add))

            for st in (Step(seg["ao"], j, None) for j in range(4)):
                j = st.j
                split_lo(dve, st)
                if j == 0:
                    for h in range(2):
                        hb = slice(4 * h, 4 * h + 4)
                        dve.wait_ge(s_.ea_done, 4 * h + 4)
                        dve.wait_ge(s_.th_done, 4 * h + 4)
                        ch(dve.tensor_tensor(MU[:, hb], RR[:, hb], RR[:, hb], ALU.mult))
                        ch.wait(dve)
                        dve.scalar_tensor_tensor(out=MU[:, hb], in0=MU[:, hb], scalar=1.0, in1=TH[:, hb], op0=ALU.add,
                                                 op1=ALU.mult).then_inc(s_.mu_ready, 1)
                dve.wait_ge(mm_done, st.count())
                dve.tensor_tensor(MIX[:, 2 * j:2 * j + 2], bank(st), GAB[:, 2 * j:2 * j + 2], ALU.mult).then_inc(freed[st.slot], 1)
                if j == 1:
                    scan()
                if j == 2:
                    dve.wait_ge(s_.gl_done, 1)
                    for p in range(4):
                        ch.wait(dve, ch.n - 6 + 2 * p)
                        blk = slice(2 * p, 2 * p + 2)
                        dve.tensor_tensor(XN[:, blk], XN[:, blk], GR[:, blk], ALU.mult).then_inc(s_.hs_ready, 1)
            for p in range(4):
                blk = slice(2 * p, 2 * p + 2)
                dve.wait_ge(s_.yh_done, p + 1)
                dve.tensor_tensor(XL[:, blk], XN[:, blk], XH[:, blk].bitcast(F32), ALU.subtract).then_inc(s_.y_done, 1)

            def mix_lo(p):
                blk = slice(2 * p, 2 * p + 2)
                dve.wait_ge(s_.mh_done, p + 1)
                dve.tensor_tensor(OL[:, blk], MIX[:, blk], OH[:, blk].bitcast(F32), ALU.subtract).then_inc(s_.ml_done, 1)

            for st in (Step(seg["ro"], j, None) for j in range(4)):
                blk = slice(2 * st.j, 2 * st.j + 2)
                split_lo(dve, st)
                dve.wait_ge(mm_done, st.count())
                dve.tensor_tensor(MU[:, blk], bank(st), GAB[:, 8 + 2 * st.j:10 + 2 * st.j], ALU.mult).then_inc(freed[st.slot], 1)
                dve.wait_ge(freed[st.slot], st.base // SLOTS + 1)
                dve.tensor_tensor(MIX[:, blk], MIX[:, blk], MU[:, blk], ALU.add).then_inc(s_.mix_ready, 1)
                if st.j:
                    mix_lo(st.j - 1)
            mix_lo(3)

            def residual(name):
                for st in (Step(seg[name], j, None) for j in range(4)):
                    split_lo(dve, st)
                    hb = H[:, 2 * st.j:2 * st.j + 2]
                    dve.wait_ge(mm_done, st.count())
                    dve.tensor_tensor(hb, hb, bank(st), ALU.add).then_inc(freed[st.slot], 1)

            residual("wo")
            norm_dve(dve, ch, 1)

            def up(st):
                split_lo(dve, st)
                dve.wait_ge(s_.sg_done, st.local())
                dve.tensor_tensor(HP[:, st.slot, 0:TOK], PS[:, st.slot, TOK:512], SG[:, st.slot, 0:TOK], ALU.mult).then_inc(freed[st.slot], 1)
                if st.i is not None or st.j:
                    hidden_lo(dve, st, 1, 0)
            steps(dve, seg["fi"], up, head=1)
            hidden_lo(dve, Step(seg["fi"], seg["fi"].n, None), 1, 0)
            steps(dve, seg["fo"], lambda st: split_lo(dve, st))
            add_rows(dve, seg["fo"], 0)
            norm_dve(dve, ch, 2)
            norm_dve(dve, ch, 3)

            def taps(st):
                for t in range(3):
                    for b in range(2):
                        blk = st.rel_at(-1) * 2 + b
                        if t == 0:
                            dve.wait_ge(s_.tap0, st.local(b - 3, 2))
                        else:
                            dve.wait_ge(s_.tapped, st.local(2 * t + b - 13, 6))
                        y = QKV[:, bass.ds(blk, 1), :]
                        dve.scalar_tensor_tensor(out=y, in0=UQ[:, bass.ds(blk, 1), t + 1:t + 1 + TOK],
                                                 scalar=vec("dn_conv_w_2", blk + 24 * (t + 1)), in1=y,
                                                 op0=ALU.mult, op1=ALU.add).then_inc(s_.tapped, 1)

            def per_head(t, g=None):
                return t[:, :, None].to_broadcast([P, 4, P])

            def dq(st):
                split_lo(dve, st)
                if st.i is None and st.j == 0:
                    dve.wait_ge(s_.beta_done, 1)
                    dve.wait_ge(s_.row_in, 48)
                    ch(dve.tensor_tensor(SMALL[:, 0].rearrange("p (c h) -> p c h", c=TT),
                                         PS[:, 3, 256:288].rearrange("p (c x) -> p c x", c=TT)[:, :, 8:16],
                                         DTB[:, None, :].to_broadcast([P, TT, 8]), ALU.add))
                    sp = softplus(None, 16, 3, 1)
                    ch(dve.tensor_tensor(GT[:].rearrange("p (c h) -> p c h", c=TT), sp.rearrange("p (c h) -> p c h", c=TT),
                                         AROW[:, None, :].to_broadcast([P, TT, 8]), ALU.mult))
                    ch.wait(dve)
                    dve.tensor_scalar(GT[:], GT[:], -1.0, None, ALU.mult).then_inc(s_.g_ready, 1)
                if st.i is None and st.j == 1:
                    dve.wait_ge(s_.gc_sum, 1)
                    dve.tensor_copy(GC[:], PS[:, 3, 320:336]).then_inc(s_.gc_done, 1)
                    dve.wait_ge(s_.sm_ready, 4)
                    dve.wait_ge(s_.beta_done, 1)
                    ch(dve.tensor_tensor(BEG[:], BETA[:, 8:16], EGC[:, 8:16], ALU.mult))
                if st.i is None and st.j == 0:
                    dve.wait_ge(s_.on, 1)
                read_out(st, UQ[:, bass.ds(st.rel * 2, 2), 3:TOK + 3])
                if st.i is not None or st.j:
                    taps(st)
            steps(dve, seg["dq"], dq, head=2)
            for st in (Step(seg["dz"], j, None) for j in range(4)):
                split_lo(dve, st)
                if st.j == 0:
                    taps(Step(seg["dq"], seg["dq"].n, None))

            for u in range(8):
                blk = slice(2 * u, 2 * u + 2)
                dve.wait_ge(s_.l2sd, u + 1)
                ch(dve.reciprocal(RN[:, blk], RN[:, blk]))
                ch.wait(dve)
                dve.scalar_tensor_tensor(out=QKV[:, blk], in0=QKV[:, blk], scalar=P ** -0.5 if u < 4 else 1.0, in1=RN[:, blk],
                                         op0=ALU.mult, op1=ALU.mult).then_inc(s_.l2done, 1)

            def four(b):
                return PS[:, b, :].rearrange("p (n i) -> p n i", n=4)

            GKB = (0, 1, 2, 7)
            for g in range(4):
                r = slice(4 * g, 4 * g + 4)
                dve.wait_ge(s_.b_done, g + 1)
                ch(dve.tensor_tensor(D1G[:, r], NEGL[:, None, :].to_broadcast([P, 4, P]), four(3 + g), ALU.subtract))
                ch(dve.tensor_tensor(D2G[:, r], NEGU[:, None, :].to_broadcast([P, 4, P]), four(3 + g), ALU.add))
                ch.wait(dve, ch.n - 1)
                dve.tensor_tensor(D1G[:, r], D1G[:, r], per_head(GC[:, r]), ALU.add).then_inc(s_.dt_ready, 1)
                ch.wait(dve)
                dve.tensor_tensor(D2G[:, r], D2G[:, r], per_head(GC[:, r]), ALU.subtract).then_inc(s_.dt_ready, 1)
            for g in range(4):
                r = slice(4 * g, 4 * g + 4)
                dve.wait_ge(s_.d_done, 2 * g + 2)
                dve.wait_ge(s_.gk_done, g + 1)
                ch(dve.tensor_tensor(AM[:, r], D1G[:, r], four(GKB[g]), ALU.mult))
                dve.wait_ge(s_.kq_done, g + 1)
                ch(dve.tensor_tensor(AT[:, r], D2G[:, r], four(3 + g), ALU.mult))
                if g < 2:
                    ch(dve.tensor_copy(LAST[:, r], D2G[:, r, P - 1:P].rearrange("p n i -> p (n i)")))
                else:
                    dve.wait_ge(s_.gl2, g - 1)
                    q = QKV[:, 4 * (g - 2):4 * (g - 2) + 4, P:TOK]
                    dve.tensor_tensor(q, q, D1[:], ALU.mult).then_inc(s_.qd_done, 1)
                ch.wait(dve, ch.n - (1 if g >= 2 else 2))
                dve.tensor_tensor(AM[:, r], AM[:, r], per_head(BETA[:, r]), ALU.mult).then_inc(s_.at_done, 1)
            ident4 = IDENT[:, None, :].to_broadcast([P, 4, P])
            for g in range(4):
                r = slice(4 * g, 4 * g + 4)
                dve.wait_ge(s_.c_done, g + 1)
                dve.tensor_tensor(TX[:, r], ident4, CM[:, r], ALU.subtract).then_inc(s_.y_out, 1)
                dve.wait_ge(s_.vt_done, g + 1)
                dve.tensor_tensor(TY[:, r], ident4, four(g), ALU.subtract).then_inc(s_.y_out, 1)
            for n in range(24):
                r = slice(4 * (n % 4), 4 * (n % 4) + 4)
                dve.wait_ge(s_.q_done, n + 1)
                if n < 20:
                    dve.tensor_tensor(TX[:, r], TX[:, r], four(2 + n % 2), ALU.subtract).then_inc(s_.y_out, 1)
                dve.tensor_tensor(TY[:, r], TY[:, r], four(4 + n % 2), ALU.subtract).then_inc(s_.y_out, 1)
                if n < 8:
                    dve.wait_ge(s_.tr_done, n + 1)
                    out, by = (VB[:, r], BETA[:, r]) if n < 4 else (KD[:, r], LAST[:, r]) if n < 6 else \
                        (KBT[:, 4 * (n - 6):4 * (n - 6) + 4], BEG[:, 4 * (n - 6):4 * (n - 6) + 4])
                    dve.tensor_tensor(out, four(6 + n % 2), per_head(by), ALU.mult).then_inc(s_.vt_out, 1)
            for g in range(2):
                dve.wait_ge(s_.vn0, g + 1)
                dve.tensor_copy(VN[:, 4 * g:4 * g + 4], four(6 + g)).then_inc(s_.vn0_out, 1)
            for g in range(2):
                dve.wait_ge(s_.s_done, g + 1)
                dve.tensor_copy(ST[:, 4 * g:4 * g + 4], four(2 + g)).then_inc(s_.s_out, 1)
            for g in range(2):
                dve.wait_ge(s_.vn1, g + 1)
                dve.tensor_copy(VN[:, 8 + 4 * g:12 + 4 * g], four(4 + g)).then_inc(s_.vn1_out, 1)
            OB = (6, 7, 0, 1)
            for u in range(4):
                dve.wait_ge(s_.o_done, u + 1)
                dve.tensor_copy(OD[:, 2 * u:2 * u + 2], two(PS[:, OB[u], :])).then_inc(s_.o_out, 1)
            for u in range(4):
                blk = slice(2 * u, 2 * u + 2)
                dve.wait_ge(s_.osd, u + 1)
                ch(dve.reciprocal(RN[:, blk], RN[:, blk]))
                ch.wait(dve)
                ch(dve.scalar_tensor_tensor(out=OD[:, blk], in0=OD[:, blk], scalar=vec("dn_out_norm_g_2", 0), in1=RN[:, blk],
                                            op0=ALU.mult, op1=ALU.mult))
                ch.wait(dve)
                dve.tensor_tensor(OD[:, blk], OD[:, blk], ZS[:, blk], ALU.mult).then_inc(s_.on2, 1)
            for u in range(4):
                blk = slice(2 * u, 2 * u + 2)
                dve.wait_ge(s_.oo, u + 1)
                dve.tensor_tensor(XL[:, blk], OD[:, blk], XH[:, blk].bitcast(F32), ALU.subtract).then_inc(s_.yy, 1)
            residual("do")

            def mlp(layer):
                norm_dve(dve, ch, 4 + 2 * layer)

                def square(st):
                    split_lo(dve, st)
                    dve.wait_ge(freed[st.slot], st.uses())
                    dve.tensor_tensor(HP[:, st.slot], SG[:, st.slot], SG[:, st.slot], ALU.mult).then_inc(s_.hp_done, 1)
                    if st.i is not None or st.j:
                        hidden_lo(dve, st, 2, HBASE[f"u{layer}"])
                u = seg[f"u{layer}"]
                steps(dve, u, square, head=1)
                hidden_lo(dve, Step(u, u.n, None), 2, HBASE[f"u{layer}"])
                w = seg[f"w{layer}"]
                steps(dve, w, lambda st: split_lo(dve, st), tail=SLOTS - 1 if layer else 0)
                add_rows(dve, w, 1 + layer)
                norm_dve(dve, ch, 5 + 2 * layer)

            mlp(0)
            steps(dve, seg["mv"], v)
            for t in range(11):
                if t >= 3 and t % 2:
                    attn_shift(dve, ch, 8 + (t - 3) // 2)
                if t < 8:
                    st = Step(seg["mq"], t, None)
                    split_lo(dve, st)
                if t >= 3 and t % 2:
                    attn_scale(dve, ch, 8 + (t - 3) // 2)
                if t < 8:
                    read_out(st, QK[:, (t % 2) * 8 + (t // 2) * 2:(t % 2) * 8 + (t // 2) * 2 + 2])
                if t >= 4 and t % 2 == 0:
                    attn_ol(dve, 8 + (t - 4) // 2)
            residual("mo")
            mlp(1)

        @block.tensor
        def _(pe):
            pe.wait_ge(s_.pool, 1)
            norm_pe(pe, 0)

            def xin(m):
                return (s_.xl_ready, 4 * split_no[m])

            def times_x(m):
                return lambda st: multiply(pe, st, XH, XL, xin(m) if st.i is None and st.j == 0 else None)

            def qk(st):
                multiply(pe, st, XH, XL, xin(0) if st.i is None and st.j == 0 else None)
                if st.i is None and st.j == 2:
                    pe.wait_ge(s_.bias_masked, 1)
                    pe.wait_ge(s_.flip_ready, 1)
                    for n in range(8):
                        if n >= 3:
                            pe.wait_ge(s_.bias_ready, n - 2)
                        pe.matmul(two(PS[:, 5 + n % 3, :]), FLIP[:], BREV[:, 2 * n:2 * n + 2], start=True, stop=True).then_inc(s_.bias_turned, 1)
            steps(pe, seg["qk"], qk, head=SLOTS)
            steps(pe, seg["v"], lambda st: multiply(pe, st, XH, XL, tokens_out=True))
            c = seg["xg"].first - 1
            pe.wait_ge(freed[c % SLOTS], c // SLOTS + 1)
            pe.wait_ge(s_.const, 2)
            attn_scores(pe, 0)
            for st in (Step(seg["xg"], j, None) for j in range(8)):
                multiply(pe, st, XH, XL)
                if st.j:
                    attn_pv(pe, st.j - 1)
                attn_turn(pe, st.j)
                if st.j < 7:
                    attn_scores(pe, st.j + 1)
            pe.wait_ge(s_.wri_in, 64)
            for st in (Step(seg["gab"], j, None) for j in range(8)):
                j = st.j
                multiply(pe, st, XH, XL)
                if j == 0:
                    attn_pv(pe, 7)
                pe.wait_ge(s_.conv_done, j + 1)
                if j >= 2:
                    pe.wait_ge(s_.gates_done, 2 * j - 2)
                for r in range(2):
                    mm = pe.matmul(PS[:, 3 + j % 2, r * TOK:(r + 1) * TOK], WRI[:, r, j], XN[:, j], start=True, stop=True)
                mm.then_inc(s_.rg_done, 1)
            pe.wait_ge(s_.ol_done, 8)
            steps(pe, seg["ao"], lambda st: multiply(pe, st, OH, OL))
            steps(pe, seg["ro"], lambda st: multiply(pe, st, XH, XL, (s_.y_done, 0) if st.j == 0 else None))
            steps(pe, seg["wo"], lambda st: multiply(pe, st, OH, OL, (s_.ml_done, 0) if st.j == 0 else None))
            norm_pe(pe, 1)
            steps(pe, seg["fi"], times_x(1), head=1)
            banks_free(pe, seg["fo"])
            steps(pe, seg["fo"], lambda st: multiply_rows(pe, st, st.local(0, 2)), head=1, tail=1)
            norm_pe(pe, 2)
            norm_pe(pe, 3)

            pe.wait_ge(s_.row_in, 48)
            pe.wait_ge(s_.xn_ready, 4 * split_no[3] + 4)
            pe.wait_ge(s_.xl_ready, 4 * split_no[3] + 1)
            for c in range(TT):
                for k in range(KB):
                    mm = pe.matmul(PS[:, 3, 256 + 16 * c:272 + 16 * c], XN[:, k, c * P:(c + 1) * P], WBA[:, k], start=(k == 0), stop=(k == KB - 1))
            mm.then_inc(s_.ba_done, 1)

            def dq(st):
                multiply(pe, st, XH, XL, xin(3) if st.i is None and st.j == 0 else None)
                if st.i is None and st.j == 0:
                    pe.wait_ge(s_.g_ready, 1)
                    pe.wait_ge(s_.beta_done, 1)
                    pe.matmul(PS[:, 3, 320:336], TRI[:], GT[:], start=True, stop=True).then_inc(s_.gc_sum, 1)
            pe.wait_ge(s_.on, 1)
            steps(pe, seg["dq"], dq, head=1)
            steps(pe, seg["dz"], lambda st: multiply(pe, st, XH, XL))

            def four(b):
                return PS[:, b, :].rearrange("p (n i) -> p n i", n=4)

            pe.wait_ge(s_.l2sq, 1)
            for u in range(8):
                if u == 4:
                    pe.wait_ge(s_.l2sq, 2)
                    for k in range(SLOTS):
                        pe.wait_ge(freed[k], uses_upto(seg["dz"], k))
                src = XN[:, 2 * u:2 * u + 2] if u < 4 else SQK[:, 2 * u - 8:2 * u - 6]
                pe.matmul(two(PS[:, (3 + u) % 8, :]), ONES[:], src, start=True, stop=True).then_inc(s_.l2sum, 1)
            for g in range(4):
                pe.wait_ge(s_.tg_done, 4 * g + 4)
                pe.matmul(four(3 + g), ONES[:], CM[:, 4 * g:4 * g + 4], start=True, stop=True).then_inc(s_.b_done, 1)
            GKB = (0, 1, 2, 7)

            def tok(block_, n):
                return QKV[:, block_ + n % 8, (n // 8) * P:(n // 8) * P + P]

            for g in range(4):
                for e in range(4):
                    n = 4 * g + e
                    mm = pe.matmul(four(GKB[g])[:, e], tok(8, n), tok(8, n), start=True, stop=True)
                mm.then_inc(s_.gk_done, 1)
            for g in range(4):
                pe.wait_ge(s_.dt_ready, 2 * g + 2)
                if g >= 2:
                    pe.wait_ge(s_.gl2, g - 1)
                for e in range(4):
                    n = 4 * g + e
                    mm = pe.matmul(four(3 + g)[:, e], tok(8, n), tok(0, n), start=True, stop=True)
                mm.then_inc(s_.kq_done, 1)
            for g in range(4):
                pe.wait_ge(s_.c_done, g + 1)
                pe.wait_ge(s_.at_done, 4)
                for e in range(4):
                    mm = pe.transpose(four(g)[:, e], CM[:, 4 * g + e], IDENT[:])
                mm.then_inc(s_.vt_done, 1)

            def level_p1(n):
                g = n % 4
                pe.wait_ge(s_.c_done, n + 5)
                pe.wait_ge(s_.y_out, 2 * (n + 1))
                if n < 2:
                    pe.wait_ge(s_.y_out, 8)
                else:
                    pe.wait_ge(s_.p1_out, n - 1)
                for e in range(4):
                    mm = pe.matmul(four(n % 2)[:, e], CM[:, 4 * g + e], TY[:, 4 * g + e], start=True, stop=True)
                mm.then_inc(s_.p1_done, 1)

            def level_q(n):
                g = n % 4
                pe.wait_ge(s_.p1_out, n + 1)
                if n >= 2:
                    pe.wait_ge(s_.y_out, 8 + (2 * (n - 1) if n - 1 <= 20 else 40 + (n - 1 - 20)))
                for e in range(4):
                    i = 4 * g + e
                    if n < 20:
                        pe.matmul(four(2 + n % 2)[:, e], P1[:, i], TX[:, i], start=True, stop=True)
                    mm = pe.matmul(four(4 + n % 2)[:, e], TX[:, i], P1[:, i], start=True, stop=True)
                mm.then_inc(s_.q_done, 1)

            def turn(u):
                if u >= 2:
                    pe.wait_ge(s_.vt_out, u - 1)
                for e in range(4):
                    n = 4 * (u % 4) + e
                    mm = pe.transpose(four(6 + u % 2)[:, e], tok(16 if u < 4 else 8, n), IDENT[:])
                mm.then_inc(s_.tr_done, 1)

            for n in range(24):
                level_p1(n)
                if n:
                    level_q(n - 1)
                if n < 8:
                    turn(n)
            level_q(23)
            for g in range(2):
                pe.wait_ge(s_.y_out, 8 + 40 + g + 1)
                pe.wait_ge(s_.vt_out, 8)
                for e in range(4):
                    n = 4 * g + e
                    mm = pe.matmul(four(6 + g)[:, e], TY[:, n], VB[:, n], start=True, stop=True)
                mm.then_inc(s_.vn0, 1)
            for g in range(2):
                pe.wait_ge(s_.y_out, 8 + 40 + g + 3)
                for e in range(4):
                    n = 4 * g + e
                    mm = pe.matmul(four(g)[:, e], KBT[:, n], TY[:, 8 + n], start=True, stop=True)
                mm.then_inc(s_.w_done, 1)
            for g in range(2):
                pe.wait_ge(s_.vn0_out, g + 1)
                for e in range(4):
                    n = 4 * g + e
                    mm = pe.matmul(four(2 + g)[:, e], KD[:, n], VN[:, n], start=True, stop=True)
                mm.then_inc(s_.s_done, 1)
            for g in range(2):
                pe.wait_ge(s_.s_out, g + 1)
                pe.wait_ge(s_.w_out, g + 1)
                for e in range(4):
                    n = 4 * g + e
                    pe.matmul(four(4 + g)[:, e], TY[:, 8 + n], VB[:, 8 + n], start=True, stop=False, skip_group_check=True)
                    mm = pe.matmul(four(4 + g)[:, e], NW[:, n], ST[:, n], start=False, stop=True, skip_group_check=True)
                mm.then_inc(s_.vn1, 1)
            OB = (6, 7, 0, 1)
            pe.wait_ge(s_.qd_done, 2)
            for u in range(4):
                pe.wait_ge(s_.vn1_out, u // 2 + 1)
                for e in range(2):
                    h = 2 * u + e
                    out = PS[:, OB[u], e * TOK:(e + 1) * TOK]
                    pe.matmul(out[:, 0:P], VN[:, h], AT[:, h], start=True, stop=True, skip_group_check=True)
                    pe.matmul(out[:, P:TOK], VN[:, 8 + h], AT[:, 8 + h], start=True, stop=False, skip_group_check=True)
                    mm = pe.matmul(out[:, P:TOK], ST[:, h], QKV[:, h, P:TOK], start=False, stop=True, skip_group_check=True)
                mm.then_inc(s_.o_done, 1)
            for u in range(4):
                pe.wait_ge(s_.osq, u + 1)
                pe.matmul(two(PS[:, 2 + u, :]), ONES[:], OSQ[:, 2 * u:2 * u + 2], start=True, stop=True).then_inc(s_.osum, 1)
            pe.wait_ge(s_.o_out, 4)
            pe.wait_ge(s_.osd, 4)
            steps(pe, seg["do"], lambda st: multiply(pe, st, XH, XL, (s_.yy, 0) if st.j == 0 else None))

            def mlp(layer):
                norm_pe(pe, 4 + 2 * layer)
                steps(pe, seg[f"u{layer}"], times_x(4 + 2 * layer), head=1)
                w = seg[f"w{layer}"]
                banks_free(pe, w)
                steps(pe, w, lambda st: multiply_rows(pe, st, st.local(HBASE[f"u{layer}"])), head=1, tail=1)
                norm_pe(pe, 5 + 2 * layer)

            mlp(0)
            steps(pe, seg["mv"], lambda st: multiply(pe, st, XH, XL, xin(5) if st.i is None and st.j == 0 else None, tokens_out=True))
            pe.wait_ge(s_.const, 3)
            for t in range(11):
                if t < 8:
                    multiply(pe, Step(seg["mq"], t, None), XH, XL)
                if t >= 4 and t % 2 == 0:
                    attn_pv(pe, 8 + (t - 4) // 2)
                if t >= 3 and t % 2:
                    attn_turn(pe, 8 + (t - 3) // 2)
                if t >= 2 and t % 2 == 0 and t <= 8:
                    c = seg["mq"].first + t - 1
                    pe.wait_ge(freed[c % SLOTS], c // SLOTS + 1)
                    attn_scores(pe, 8 + (t - 2) // 2)
            pe.wait_ge(s_.ol_done, 12)
            steps(pe, seg["mo"], lambda st: multiply(pe, st, OH, OL))
            mlp(1)


_VECTORS = [name for name, _ in VECTORS]


def kernel(**inputs):
    import numpy as np
    import concourse.bacc as bacc
    from concourse.bass_utils import run_bass_kernel_spmd

    x = {k: np.asarray(v) for k, v in inputs.items()}

    def columns(v):
        return np.ascontiguousarray(v.reshape(-1, P).T)

    arrays = {
        "x": np.ascontiguousarray(x["x"][0].T),
        "vectors": np.concatenate([columns(x[n]) for n in _VECTORS], axis=1),
        "rel_reversed": np.ascontiguousarray(x["rel_table"][0][:, ::-1]),
        "dn_a_log": x["dn_a_log_2"], "dn_dt_bias": x["dn_dt_bias_2"],
        "w_in": x["w_in"][0], "w_rg_r": x["w_rg_r"][0], "w_rg_i": x["w_rg_i"][0],
        "w_attn_out": x["w_attn_out"][0], "w_rnn_out": x["w_rnn_out"][0], "w_o": x["w_o"][0],
        "w_ffn_in_pairs": x["w_ffn_in"][0].reshape(D, 2, FF1 // P, P).transpose(0, 2, 1, 3).reshape(D, 2 * FF1),
        "w_ffn_out": x["w_ffn_out"][0],
        "dn_w_in": x["dn_w_in_2"][0], "dn_w_out": x["dn_w_out_2"][0],
        "mb_w_in": x["mb_w_in_2"][0], "mb_w_out": x["mb_w_out_2"][0],
        "mlp_w_up": x["mlp_w_up_2"], "mlp_w_down": x["mlp_w_down_2"],
    }
    nc = bacc.Bacc("TRN2", target_bir_lowering=False, num_devices=1)
    maps, aps = {}, {}
    for name, v in arrays.items():
        v = np.ascontiguousarray(v)
        maps[f"in_{name}"] = v
        aps[name] = nc.dram_tensor(f"in_{name}", v.shape, mybir.dt.from_np(v.dtype), kind="ExternalInput").ap()
    aps["out"] = nc.dram_tensor("out_t", (D, TOK), F32, kind="ExternalOutput").ap()
    build(nc, aps)
    r = run_bass_kernel_spmd(nc, [maps], core_ids=[0])
    return np.ascontiguousarray(r.results[0]["out_t"].T)[None]
```

```python
from contextlib import ExitStack

import concourse.bass as bass
from concourse import mybir

F32 = mybir.dt.float32
F32R = mybir.dt.float32r
ALU = mybir.AluOpType
ACT = mybir.ActivationFunctionType
AX_X = mybir.AxisListType.X

P = 128
D = 1024
TOK = 256
KB = D // P
TT = TOK // P
SLOTS = 3
CW = 2048
NCOL = CW // KB
KROWS = CW // D
FF1 = 2816
FF2 = 4096
NEG = -1.0e30
EPS = 1e-6

SEGMENTS = [
    ("qk", 8), ("v", 4), ("xg", 8), ("gab", 8), ("ao", 4), ("ro", 4), ("wo", 4),
    ("fi", FF1 // P), ("fo", FF1 // P // KROWS),
    ("dq", 12), ("dz", 4), ("do", 4), ("u0", 16), ("w0", 16),
    ("mq", 8), ("mv", 4), ("mo", 4), ("u1", 16), ("w1", 16),
]
TOTAL = sum(n for _, n in SEGMENTS)

VECTORS = [
    ("norm_mix_g", 8), ("b_merge", 16), ("conv_w", 32), ("conv_b", 8), ("b_rg_r", 8),
    ("b_rg_i", 8), ("rg_lambda", 8), ("norm_ffn_g", 8), ("final_norm_g", 8),
    ("mix_norm_g_2", 16), ("mlp_norm_g_2", 16), ("dn_conv_w_2", 96), ("dn_out_norm_g_2", 1),
    ("final_norm_g_2", 8),
]
NVEC = sum(n for _, n in VECTORS)


class Segment:
    def __init__(self, name, first, n):
        self.name, self.first, self.n = name, first, n


def plan():
    out, at = {}, 0
    for name, n in SEGMENTS:
        out[name] = Segment(name, at, n)
        at += n
    return out


class Step:

    def __init__(self, seg, j, i):
        self.seg, self.j, self.i = seg, j, i
        self.base = seg.first + j
        self.slot = self.base % SLOTS

    def _plus(self, n, per):
        return n if self.i is None else self.i * per + n

    @property
    def rel(self):
        return self._plus(self.j, SLOTS)

    def rel_at(self, off):
        return self._plus(self.j + off, SLOTS)

    def count(self, off=0):
        return self._plus(self.base + 1 + off, SLOTS)

    def local(self, off=0, per=1):
        return self._plus((self.j + 1) * per + off, SLOTS * per)

    def uses(self, ahead=0, per=1):
        return self._plus(((self.base + ahead) // SLOTS + 1) * per, per)


def steps(eng, seg, body, head=0, tail=0):
    for j in range(head):
        body(Step(seg, j, None))
    turns = (seg.n - head - tail) // SLOTS
    at = head
    if turns >= 2:
        with eng.Fori(0, turns, 1) as i:
            for j in range(SLOTS):
                body(Step(seg, head + j, i))
        at += turns * SLOTS
    for j in range(at, seg.n):
        body(Step(seg, j, None))


class Chain:

    def __init__(self, sem):
        self.sem, self.n = sem, 0

    def __call__(self, ins):
        self.n += 1
        ins.then_inc(self.sem, 1)
        return self.n

    def wait(self, eng, n=None):
        eng.wait_ge(self.sem, self.n if n is None else n)


def build(nc, a):
    seg = plan()
    K1 = 1024
    base = -(-nc.sbuf_base // 64) * 64

    def sb(name, shape, dt, kib):
        return nc.alloc_sbuf_tensor_at(name, shape, dt, offset=base + int(kib * K1) // 32 * 32)

    RC = sb("RC", [P, 4], F32, 111.3)
    SDC = sb("SDC", [P, 4], F32, 111.4)
    G23 = sb("G23", [P, KB], F32, 111.5)
    W2 = sb("W2", [P, KB, 2], F32, 111.6)
    Z = 111.75
    RAW = sb("RAW", [P, SLOTS, CW], F32, 0)
    WH = sb("WH", [P, SLOTS, CW], F32R, 24)
    WL = sb("WL", [P, SLOTS, CW], F32R, 48)
    H = sb("H", [P, KB, TOK], F32, 72)
    XH = sb("XH", [P, KB, TOK], F32R, 80)
    XL = sb("XL", [P, KB, TOK], F32R, 88)
    XN = sb("XN", [P, KB, TOK], F32, 96)
    VEC = sb("VEC", [P, NVEC], F32, 104)
    IDENT = sb("IDENT", [P, P], F32, 105)
    FLIP = sb("FLIP", [P, P], F32, Z + 88.25)
    ONES = sb("ONES", [P, P], F32, 105.5)
    NALI = sb("NALI", [P, TOK], F32, 106)
    RH = sb("RH", [P, TOK], F32, 107)
    TAP = sb("TAP", [P, 1, TOK], F32, 107)
    RSTD = sb("RSTD", [P, TOK], F32, 108)
    WBA = sb("WBA", [P, KB, 16], F32, 109)
    EPSC = sb("EPSC", [P, 1], F32, 109.5)
    SP8 = sb("SP8", [P, 8], F32, 109.6)
    NSP8 = sb("NSP8", [P, 8], F32, 109.7)
    NMX = sb("NMX", [P, 4], F32, 109.8)
    SUM = sb("SUM", [P, 4], F32, 109.9)
    RSUM = sb("RSUM", [P, 4], F32, 110)
    AROW = sb("AROW", [P, 8], F32, 110.1)
    DTB = sb("DTB", [P, 8], F32, 110.2)
    SMALL = sb("SMALL", [P, 6, 16], F32, 110.3)
    GT = sb("GT", [P, 16], F32, 110.7)
    GC = sb("GC", [P, 16], F32, 110.8)
    EGC = sb("EGC", [P, 16], F32, 110.9)
    BETA = sb("BETA", [P, 16], F32, 111)
    BEG = sb("BEG", [P, 8], F32, 111.1)
    LAST = sb("LAST", [P, 8], F32, 111.2)
    QK = sb("QK", [P, 16, TOK], F32, Z + 0)
    VT = sb("VT", [P, TT, D], F32, Z + 16)
    BIAS = sb("BIAS", [P, 16, TOK], F32, Z + 24)
    BREV = sb("BREV", [P, 16, TOK], F32, Z + 40)
    OH = sb("OH", [P, KB, TOK], F32R, Z + 40)
    OL = sb("OL", [P, KB, TOK], F32R, Z + 48)
    XR = sb("XR", [P, KB, TOK + 3], F32, Z + 56)
    GR = sb("GR", [P, KB, TOK], F32, Z + 64.25)
    WRI = sb("WRI", [P, 2, KB, P], F32, Z + 72.25)
    PR = sb("PR", [P, 2, 384], F32, Z + 80.25)
    PTM = sb("PTM", [P, 4, 2, 384], F32, Z + 24)
    PT = sb("PT", [P, 2, 384], F32, Z + 83.25)
    EXT = sb("EXT", [16, 384], F32, Z + 86.25)
    GAB = sb("GAB", [P, 16, TOK], F32, Z + 0)
    RR = sb("RR", [P, KB, TOK], F32, Z + 24)
    RI = sb("RI", [P, KB, TOK], F32, Z + 32)
    TH = sb("TH", [P, KB, TOK], F32, Z + 56)
    MIX = sb("MIX", [P, KB, TOK], F32, Z + 16)
    MU = sb("MU", [P, KB, TOK], F32, Z + 80.25)
    HH = sb("HH", [P, 32, TOK], F32R, Z + 0)
    HL = sb("HL", [P, 32, TOK], F32R, Z + 32)
    SG = sb("SG", [P, SLOTS, 512], F32, Z + 64)
    HP = sb("HP", [P, SLOTS, 512], F32, Z + 70)
    UQ = sb("UQ", [P, 24, TOK + 3], F32, Z + 0)
    QKV = sb("QKV", [P, 24, TOK], F32, Z + 24.5)
    ZS = sb("ZS", [P, KB, TOK], F32, Z + 48.5)
    AM = sb("AM", [P, 16, P], F32, Z + 56.5)
    CM = sb("CM", [P, 16, P], F32, Z + 64.5)
    AT = sb("AT", [P, 16, P], F32, Z + 72.5)
    RNC = sb("RNC", [P, 32], F32, Z + 82.5)
    RNS = sb("RNS", [P, 32], F32, Z + 82.75)
    TRI = sb("TRI", [P, P], F32, Z + 90)
    NEGL = sb("NEGL", [P, P], F32, Z + 90.5)
    NEGU = sb("NEGU", [P, P], F32, Z + 91)
    LM = sb("LM", [P, 7, P], F32, Z + 91.5)
    SQK = sb("SQK", [P, KB, TOK], F32, Z + 64.5)
    TAP2 = sb("TAP2", [P, 2, TOK], F32, Z + 80.5)
    TX = sb("TX", [P, 16, P], F32, Z + 0)
    TY = sb("TY", [P, 16, P], F32, Z + 8)
    P1 = sb("P1", [P, 16, P], F32, Z + 16)
    VB = sb("VB", [P, 16, P], F32, 96)
    KD = sb("KD", [P, 8, P], F32, Z + 40.5)
    KBT = sb("KBT", [P, 8, P], F32, Z + 44.5)
    VN = sb("VN", [P, 16, P], F32, Z + 0)
    ST = sb("ST", [P, 8, P], F32, Z + 64.5)
    NW = sb("NW", [P, 8, P], F32, Z + 68.5)
    OD = sb("OD", [P, KB, TOK], F32, Z + 16)
    DOH = sb("DOH", [P, KB, TOK], F32R, Z + 32.5)
    DOL = sb("DOL", [P, KB, TOK], F32R, Z + 8)
    OSQ = sb("OSQ", [P, KB, TOK], F32, Z + 56.5)

    ext_dram = nc.dram_tensor("bias_rows", [16, 384], F32, kind="Internal").ap()

    vec_at, at = {}, 0
    for name, n in VECTORS:
        vec_at[name] = at
        at += n

    def vec(name, j):
        return VEC[:, bass.ds(j + vec_at[name], 1)]

    with ExitStack() as ctx:
        PS = ctx.enter_context(nc.psum_tensor("PS", [P, 8, 512], F32))

        def sem(name):
            return ctx.enter_context(nc.semaphore(name))

        raw_in = [sem(f"raw_in{s}") for s in range(SLOTS)]
        x_in = [sem(f"x_in{p}") for p in range(4)]
        hi_done = sem("hi_done")
        lo_done = sem("lo_done")
        mm_done = sem("mm_done")
        freed = [sem(f"freed{s}") for s in range(SLOTS)]
        names = """rows_scaled vec_in wri_in kq_done tr_done on2 tab_in ext_ready ext_out bias_in row_in out_done const wri_zero
          flip_ready bias_masked bias_turned bias_ready sq_done sq_added sum_done sd_done second_in rc_ready
          rows_ready rh_ready xh_ready xl_ready rows_done h4 h2 prep gab_done sg_in zs_done xout scored
          shifted exped scaled turned pt_ready pv_done oh_done ol_done conv_done rg_done gates_done th_done
          ea_done mu_ready rt_done ri_done scanned gl_done hs_ready yh_done y_done mix_ready mh_done ml_done
          dve pool sg_done hp_done hh_done hl_done tap0 tap1 tap2 tap3 tapped silu_done ba_done beta_done
          ey_done g_ready gc_sum gc_done sm_ready l2sq l2sum l2sd rnc unit_rows l2done b_done b_read dt_ready
          d_done ab_done gk_done a_done at_done ct_done vt_out c_done p1_done p1_out q_done x_done x_out
          tx_in ty_out zg_done vn0 vn0_out s_done s_out w_done w_out vn1 vn1_out o_done o_out osq osum osd
          orows gated uq_zero yy oo""".split()
        s = {n: sem(n) for n in names}
        s_ = type("Sems", (), s)
        block = ctx.enter_context(nc.Block())

        def cols(w, c0, n=NCOL):
            return w.rearrange("(k p) n -> p k n", p=P)[:, :, bass.ds(c0, n)]

        def rows(w, r0):
            return w.rearrange("(k p) n -> p k n", p=P)[:, bass.ds(r0, KROWS), :]

        def source(name, rel):
            if name in ("qk", "v", "xg", "gab"):
                first = {"qk": 0, "v": 2048, "xg": 3072, "gab": 5120}[name]
                return cols(a["w_in"], rel * NCOL + first)
            if name == "dq" or name == "dz":
                return cols(a["dn_w_in"], rel * NCOL + (3072 if name == "dz" else 0))
            if name == "mv":
                return cols(a["mb_w_in"], rel * NCOL + 2048)
            if name == "mq":
                return cols(a["mb_w_in"], (rel % 2) * D + (rel // 2) * NCOL)
            if name in ("u0", "u1"):
                return cols(a["mlp_w_up"][int(name[1])], rel * NCOL)
            if name in ("w0", "w1"):
                return rows(a["mlp_w_down"][int(name[1])], rel * KROWS)
            if name == "fo":
                return rows(a["w_ffn_out"], rel * KROWS)
            w = {"fi": "w_ffn_in_pairs", "ao": "w_attn_out", "ro": "w_rnn_out", "wo": "w_o", "do": "dn_w_out", "mo": "mb_w_out"}
            return cols(a[w[name]], rel * NCOL)

        def fetch(eng, st):
            if st.i is not None or st.base >= SLOTS:
                eng.wait_ge(lo_done, st.count(-SLOTS))
            name = st.seg.name
            k = KROWS if name in ("fo", "w0", "w1") else KB
            dst = RAW[:, st.slot, :].rearrange("p (k n) -> p k n", k=k)
            eng.dma_start(dst, source(name, st.rel)).then_inc(raw_in[st.slot], 16)

        def slot_of(st, ahead):
            return (st.base + ahead) % SLOTS

        def ahead_of(st):
            return None if st.i is None and st.base + SLOTS - 1 >= TOTAL else SLOTS - 1

        def split_hi(act, st, ahead="next"):
            n = ahead_of(st) if ahead == "next" else ahead
            if n is None:
                return
            k = slot_of(st, n)
            act.wait_ge(raw_in[k], st.uses(n, 16))
            if st.i is not None or st.base + n >= SLOTS:
                act.wait_ge(mm_done, st.count(n - SLOTS))
            act.activation(WH[:, k], RAW[:, k], ACT.Copy).then_inc(hi_done, 1)

        def split_lo(dve, st, ahead="next"):
            n = ahead_of(st) if ahead == "next" else ahead
            if n is None:
                return
            k = slot_of(st, n)
            dve.wait_ge(hi_done, st.count(n))
            dve.tensor_tensor(WL[:, k], RAW[:, k], WH[:, k].bitcast(F32), ALU.subtract).then_inc(lo_done, 1)

        def product(pe, out, wh, wl, xh, xl, start, stop):
            pe.matmul(out, wh, xh, start=start, stop=False, skip_group_check=True)
            pe.matmul(out, wh, xl, start=False, stop=False, skip_group_check=True)
            return pe.matmul(out, wl, xh, start=False, stop=stop, skip_group_check=True)

        def bank_free(pe, st):
            if st.i is not None or st.base >= SLOTS:
                pe.wait_ge(freed[st.slot], st.uses(-SLOTS))

        def multiply(pe, st, xh, xl, pieces=None, tokens_out=False, between=None):
            pe.wait_ge(lo_done, st.count())
            bank_free(pe, st)
            h = WH[:, st.slot].rearrange("p (k n) -> p k n", k=KB)
            l = WL[:, st.slot].rearrange("p (k n) -> p k n", k=KB)
            for b in range(2):
                if b and between:
                    between()
                out = PS[:, st.slot, b * TOK:(b + 1) * TOK]
                part = slice(b * P, b * P + P)
                for k in range(KB):
                    if pieces is not None and b == 0 and k % 2 == 0:
                        pe.wait_ge(pieces[0], pieces[1] + k // 2 + 1)
                    if tokens_out:
                        mm = product_t(pe, out, xh[:, k, part], xl[:, k, part], h[:, k], l[:, k], k == 0, k == KB - 1)
                    else:
                        mm = product(pe, out, h[:, k, part], l[:, k, part], xh[:, k], xl[:, k], k == 0, k == KB - 1)
            mm.then_inc(mm_done, 1)

        def product_t(pe, out, xh, xl, wh, wl, start, stop):
            pe.matmul(out, xh, wh, start=start, stop=False, skip_group_check=True)
            pe.matmul(out, xh, wl, start=False, stop=False, skip_group_check=True)
            return pe.matmul(out, xl, wh, start=False, stop=stop, skip_group_check=True)

        def multiply_rows(pe, st, ready):
            pe.wait_ge(lo_done, st.count())
            pe.wait_ge(s_.hl_done, ready)
            h = WH[:, st.slot].rearrange("p (k n) -> p k n", k=KROWS)
            l = WL[:, st.slot].rearrange("p (k n) -> p k n", k=KROWS)
            first = st.i is None and st.j == 0
            last = st.i is None and st.j == st.seg.n - 1
            order = [(k, b) for k in range(KROWS) for b in range(KB)]
            if last:
                order = [(k, b) for b in range(KB) for k in range(KROWS)]
            for k, b in order:
                xh = HH[:, bass.ds(st.rel * KROWS + k, 1), :].rearrange("p k t -> p (k t)")
                xl = HL[:, bass.ds(st.rel * KROWS + k, 1), :].rearrange("p k t -> p (k t)")
                mm = product(pe, PS[:, b // 2, (b % 2) * TOK:(b % 2 + 1) * TOK],
                             h[:, k, b * P:(b + 1) * P], l[:, k, b * P:(b + 1) * P], xh, xl,
                             first and k == 0 and b % 2 == 0, last and k == KROWS - 1)
                if last and b % 2 and b < KB - 1 and k == KROWS - 1:
                    mm.then_inc(s_.rows_done, 1)
            mm.then_inc(mm_done, 1)

        def uses_upto(sg, k):
            return sum(1 for c in range(sg.first + sg.n) if c % SLOTS == k)

        def banks_free(pe, sg):
            for k in range(SLOTS):
                pe.wait_ge(freed[k], uses_upto(sg, k) - sum(1 for c in range(sg.first, sg.first + sg.n) if c % SLOTS == k))

        SOURCE = [None, "wo", "fo", "do", "w0", "mo", "w1"]
        FINAL = 6
        SUMS_AT = [2, 1, 1, 2, 2, 2]
        ROWS_AT = [3, 2, 2, 5, 3, 5]
        h4_no = {"fo": 1, "w0": 2, "w1": 3}

        def weight(m, j):
            if m == 2:
                return G23[:, j:j + 1]
            return vec(*[("norm_mix_g", j), ("norm_ffn_g", j), None, ("mlp_norm_g_2", j), ("mix_norm_g_2", 8 + j),
                         ("mlp_norm_g_2", 8 + j), ("final_norm_g_2", j)][m])

        def wait_h(eng, m, p):
            src = SOURCE[m]
            if src is None:
                eng.wait_ge(x_in[p], 16)
            elif src in h4_no:
                if p < SLOTS:
                    eng.wait_ge(freed[p], uses_upto(seg[src], p))
                else:
                    eng.wait_ge(s_.h4, h4_no[src])
            else:
                c = seg[src].first + p
                eng.wait_ge(freed[c % SLOTS], c // SLOTS + 1)

        def squares(act, m, p):
            act.activation(XN[:, 2 * p:2 * p + 2], H[:, 2 * p:2 * p + 2], ACT.Square).then_inc(s_.sq_done, 1)

        def norm_high(act, m, p, squares=squares):
            wait_h(act, m, p)
            if m != FINAL:
                for j in (2 * p, 2 * p + 1):
                    ins = act.activation(XH[:, j], H[:, j], ACT.Copy, scale=weight(m, j))
                ins.then_inc(s_.xh_ready, 1)
            if squares:
                squares(act, m, p)

        def norm_low(dve, m, p):
            dve.wait_ge(s_.xh_ready, 4 * m + p + 1)
            for j in (2 * p, 2 * p + 1):
                ins = dve.scalar_tensor_tensor(out=XL[:, j], in0=H[:, j], scalar=weight(m, j), in1=XH[:, j].bitcast(F32),
                                               op0=ALU.mult, op1=ALU.subtract)
            ins.then_inc(s_.xl_ready, 1)

        def norm_add(pool, pc, m):
            pool.wait_ge(s_.sq_done, 4 * m + 2)
            pc(pool.tensor_tensor(XN[:, 0:2], XN[:, 0:2], XN[:, 2:4], ALU.add))
            pool.wait_ge(s_.sq_done, 4 * m + 4)
            pc(pool.tensor_tensor(XN[:, 4:6], XN[:, 4:6], XN[:, 6:8], ALU.add))
            pc.wait(pool)
            pc(pool.tensor_tensor(XN[:, 0:2], XN[:, 0:2], XN[:, 4:6], ALU.add))
            pc.wait(pool)
            pool.tensor_tensor(XN[:, 0], XN[:, 0], XN[:, 1], ALU.add).then_inc(s_.sq_added, 1)

        def norm_sums(pe, m):
            if m == FINAL:
                for j in range(KB):
                    if j % 2 == 0:
                        pe.wait_ge(s_.sq_done, 4 * m + j // 2 + 1)
                    mm = pe.matmul(PS[:, 4, 0:TOK], ONES[:], XN[:, j], start=(j == 0), stop=(j == KB - 1))
            elif m == 2:
                pe.wait_ge(s_.sq_done, 4 * m + 4)
                for c in range(TT):
                    for j in range(KB):
                        mm = pe.matmul(PS[:, 4, 2 * c:2 * c + 2], XN[:, j, c * P:(c + 1) * P], W2[:, j],
                                       start=(j == 0), stop=(j == KB - 1))
            else:
                pe.wait_ge(s_.sq_added, m + 1 - (m > 2))
                for c in range(TT):
                    mm = pe.matmul(PS[:, 4, c:c + 1], XN[:, 0, c * P:(c + 1) * P], ONES[:, 0:1], start=True, stop=True)
            mm.then_inc(s_.sum_done, 1)

        def norm_root(act, m):
            act.wait_ge(s_.sum_done, m + 1)
            if m == 2:
                act.activation(SDC[:, 0:2], PS[:, 4, 0:4].rearrange("p (c x) -> p c x", x=2)[:, :, 0], ACT.Sqrt,
                               bias=EPSC[:], scale=1.0 / D).then_inc(s_.sd_done, 1)
                act.wait_ge(s_.second_in, 1)
                act.activation(SDC[:, 2:4], SDC[:, 2:4], ACT.Sqrt, bias=EPSC[:], scale=1.0 / D).then_inc(s_.sd_done, 1)
            elif m == FINAL:
                act.activation(RH[:], PS[:, 4, 0:TOK], ACT.Sqrt, bias=EPSC[:], scale=1.0 / D).then_inc(s_.sd_done, 1)
            else:
                act.activation(SDC[:, 0:2], PS[:, 4, 0:2], ACT.Sqrt, bias=EPSC[:], scale=1.0 / D).then_inc(s_.sd_done, 1)

        def norm_rows(pe, m):
            pe.wait_ge(s_.rc_ready, m + 1)
            for c in range(4 if m == 2 else 2):
                mm = pe.transpose(PS[:, 5, c * P:(c + 1) * P], RC[:, c:c + 1].to_broadcast([P, P]), IDENT[:])
            mm.then_inc(s_.rows_ready, 1)

        def norm_point(pe, m, at):
            if at == SUMS_AT[m]:
                norm_sums(pe, m)
            if at == ROWS_AT[m]:
                norm_rows(pe, m)

        def norm_scale(dve, ch, m):
            if m == 2:
                dve.wait_ge(s_.sd_done, 3)
                ch(dve.reciprocal(RC[:, 2:4], SDC[:, 0:2]))
                ch.wait(dve)
                ch(dve.tensor_tensor(SDC[:, 2:4], RC[:, 2:4], RC[:, 2:4], ALU.mult))
                ch.wait(dve)
                dve.tensor_tensor(SDC[:, 2:4], SDC[:, 2:4], PS[:, 4, 0:4].rearrange("p (c x) -> p c x", x=2)[:, :, 1],
                                  ALU.mult).then_inc(s_.second_in, 1)
                dve.wait_ge(s_.sd_done, 4)
                ch(dve.reciprocal(RC[:, 0:2], SDC[:, 2:4]))
                ch.wait(dve)
                dve.tensor_tensor(RC[:, 0:2], RC[:, 0:2], RC[:, 2:4], ALU.mult).then_inc(s_.rc_ready, 1)
                dve.wait_ge(s_.rows_ready, 3)
                dve.tensor_copy(RH[:], PS[:, 5, TOK:512]).then_inc(s_.rh_ready, 1)
            else:
                dve.wait_ge(s_.sd_done, m + 1 + (m > 2))
                dve.reciprocal(RC[:, 0:2], SDC[:, 0:2]).then_inc(s_.rc_ready, 1)
                dve.wait_ge(s_.rows_ready, m + 1)
            ch(dve.tensor_copy(RSTD[:], PS[:, 5, 0:TOK]))
            ch.wait(dve)
            if m in (3, 5):
                ch(dve.tensor_tensor(RSTD[:], RSTD[:], RSTD[:], ALU.mult))
                ch.wait(dve)

        def by_rows(n):
            return RSTD[:, None, :].to_broadcast([P, n, TOK])

        def scale_rows(dve, sg, m):
            for b in range(4):
                if b < 3:
                    dve.wait_ge(s_.rows_done, 3 * h4_no[sg.name] - 2 + b)
                else:
                    dve.wait_ge(mm_done, sg.first + sg.n)
                dve.tensor_tensor(XN[:, 2 * b:2 * b + 2, :], PS[:, b, :].rearrange("p (c t) -> p c t", c=2), by_rows(2),
                                  ALU.mult).then_inc(s_.rows_scaled, 1)
                if b > 1 and m != FINAL:
                    norm_low(dve, m, b - 2)
            if m != FINAL:
                norm_low(dve, m, 2)
                norm_low(dve, m, 3)

        def add_rows(pool, sg):
            for b in range(4):
                pool.wait_ge(s_.rows_scaled, 4 * h4_no[sg.name] - 3 + b)
                hb = H[:, 2 * b:2 * b + 2, :]
                ins = pool.tensor_tensor(hb, hb, XN[:, 2 * b:2 * b + 2, :], ALU.add)
                if b < SLOTS:
                    ins.then_inc(freed[b], sum(1 for c in range(sg.first, sg.first + sg.n) if c % SLOTS == b))
                else:
                    ins.then_inc(s_.h4, 1)

        SCALE = {False: 64.0 ** -0.5, True: 128.0 ** -0.5}

        OUTB = (7, 3, 4, 7)

        def heads(n):
            for e in range(2):
                if n < 8:
                    rows_, j = slice(64 * e, 64 * e + 64), n
                    yield 2 * n + e, QK[rows_, j], QK[rows_, 8 + j], slice((2 * n + e) * 64, (2 * n + e) * 64 + 64), PS[rows_, 7, 0:TOK]
                else:
                    h = 2 * (n - 8) + e
                    yield h, QK[:, h], QK[:, 8 + h], slice(h * P, h * P + P), PS[:, OUTB[n - 8], e * TOK:(e + 1) * TOK]

        def attn_scores(pe, n):
            for e, (_, q, k, _, _) in enumerate(heads(n)):
                pe.matmul(PS[:, 3 + e, 0:P], q[:, 0:P], k[:, 0:P], start=True, stop=True)
                mm = pe.matmul(PS[:, 3 + e, P:384], q[:, P:TOK], k[:, 0:TOK], start=True, stop=True)
            mm.then_inc(s_.scored, 1)

        def attn_shift(dve, ch, n):
            moba = n >= 8
            dve.wait_ge(s_.scored, n + 1)
            for e, (h, *_) in enumerate(heads(n)):
                for t, w in ((0, P), (1, TOK)):
                    cols_ = slice(P * t, P * t + w)
                    if moba:
                        bias, out = NALI[:, TOK - w:TOK], dict(in0=NALI[:, TOK - w:TOK], in1=PS[:, 3 + e, cols_])
                        k = 2.0 ** -(h + 1) / SCALE[True]
                    else:
                        out = dict(in0=PS[:, 3 + e, cols_], in1=BIAS[:, h, TOK - w:TOK])
                        k = SCALE[False]
                    ch(dve.scalar_tensor_tensor(out=PR[:, e, cols_], scalar=k, op0=ALU.mult, op1=ALU.add, **out))
            for e in range(2):
                for t, w in ((0, P), (1, TOK)):
                    ch.wait(dve, ch.n - 3)
                    ch(dve.tensor_reduce(out=NMX[:, 2 * e + t:2 * e + t + 1], in_=PR[:, e, P * t:P * t + w],
                                         axis=AX_X, op=ALU.max))
            ch.wait(dve)
            dve.tensor_scalar(NMX[:], NMX[:], -SCALE[True] if moba else -1.0, None, ALU.mult).then_inc(s_.shifted, 1)

        def attn_exp(act, n):
            act.wait_ge(s_.shifted, n + 1)
            for e in range(2):
                for t, w in ((0, P), (1, TOK)):
                    i = 2 * e + t
                    pr = PR[:, e, P * t:P * t + w]
                    act.activation(pr, pr, ACT.Exp, bias=NMX[:, i:i + 1], scale=SCALE[True] if n >= 8 else 1.0,
                                   accum_out=SUM[:, i:i + 1]).then_inc(s_.exped, 1)

        def attn_scale(dve, ch, n):
            dve.wait_ge(s_.exped, 4 * n + 4)
            ch(dve.reciprocal(RSUM[:], SUM[:]))
            ch.wait(dve)
            for e in range(2):
                for t, w in ((0, P), (1, TOK)):
                    pr = PR[:, e, P * t:P * t + w]
                    dve.tensor_scalar(pr, pr, RSUM[:, 2 * e + t:2 * e + t + 1], None, ALU.mult).then_inc(s_.scaled, 1)

        def attn_turn(pe, n):
            pe.wait_ge(s_.scaled, 4 * n + 4)
            if n:
                pe.wait_ge(s_.pt_ready, 2 * n)
            for e in range(2):
                for b in range(3):
                    mm = pe.transpose(PS[:, 5 + e, P * b:P * b + P], PR[:, e, P * b:P * b + P], IDENT[:])
            mm.then_inc(s_.turned, 1)

        def turned_to(n):
            return PT if n < 8 else PTM[:, n - 8]

        def attn_pt(act, n):
            act.wait_ge(s_.turned, n + 1)
            for e in range(2):
                act.activation(turned_to(n)[:, e], PS[:, 5 + e, 0:384], ACT.Copy).then_inc(s_.pt_ready, 1)

        def attn_pv(pe, n):
            pe.wait_ge(s_.pt_ready, 2 * n + 2)
            if n in (9, 10):
                pe.wait_ge(s_.shifted, 12)
            elif n:
                pe.wait_ge(s_.ol_done, 9 if n == 11 else n)
            for e, (_, _, _, vc, out) in enumerate(heads(n)):
                pt = turned_to(n)
                pe.matmul(out[:, 0:P], VT[:, 0, vc], pt[:, e, 0:P], start=True, stop=True, skip_group_check=True)
                pe.matmul(out[:, P:TOK], VT[:, 0, vc], pt[:, e, P:TOK], start=True, stop=False, skip_group_check=True)
                mm = pe.matmul(out[:, P:TOK], VT[:, 1, vc], pt[:, e, TOK:384], start=False, stop=True, skip_group_check=True)
            mm.then_inc(s_.pv_done, 1)

        def out_blocks(n):
            if n < 8:
                return slice(n, n + 1), PS[:, 7, 0:TOK].rearrange("p (c t) -> p c t", c=1)
            return slice(2 * (n - 8), 2 * (n - 8) + 2), PS[:, OUTB[n - 8], :].rearrange("p (c t) -> p c t", c=2)

        def attn_oh(act, n):
            act.wait_ge(s_.pv_done, n + 1)
            b, ps = out_blocks(n)
            act.activation(OH[:, b], ps, ACT.Copy).then_inc(s_.oh_done, 1)

        def attn_ol(dve, n):
            dve.wait_ge(s_.oh_done, n + 1)
            b, ps = out_blocks(n)
            dve.tensor_tensor(OL[:, b], ps, OH[:, b].bitcast(F32), ALU.subtract).then_inc(s_.ol_done, 1)

        UB = (3, 4, 6, 7, 0, 1, 2, 5)
        OB = (6, 7, 0, 1)
        RB = (2, 3, 5, 6)

        def moba_step(t):
            return Step(seg["mq"], t, None) if t < 8 else Step(seg["mv"], t - 8, None)

        def two(ap):
            return ap.rearrange("p (c t) -> p c t", c=2)

        def bank(st):
            return two(PS[:, st.slot, :])

        @block.sync
        def _(sp):
            for p in range(4):
                sp.dma_start(H[:, 2 * p:2 * p + 2], a["x"].rearrange("(j p) t -> p j t", p=P)[:, 2 * p:2 * p + 2]).then_inc(x_in[p], 16)
            for name, n in SEGMENTS:
                steps(sp, seg[name], lambda st: fetch(sp, st), head=SLOTS if name == "qk" else 0)
            for p in range(4):
                sp.wait_ge(s_.xout, p + 1)
                sp.dma_start(a["out"].rearrange("(j p) t -> p j t", p=P)[:, 2 * p:2 * p + 2], XN[:, 2 * p:2 * p + 2]).then_inc(s_.out_done, 16)
            sp.wait_ge(s_.out_done, 64)

        @block.gpsimd
        def _(pool):
            pc = Chain(s_.pool)
            pc(pool.memset(ONES[:], 1.0))
            pool.memset(EPSC[:], EPS).then_inc(s_.const, 1)
            pc(pool.memset(WRI[:], 0.0))
            pool.memset(XR[:, :, 0:3], 0.0).then_inc(s_.wri_zero, 1)
            pc(pool.memset(IDENT[:], 0.0))
            pc(pool.memset(FLIP[:], 0.0))
            pc.wait(pool)
            pool.affine_select(out=IDENT[:], in_=IDENT[:], compare_op=ALU.not_equal, fill=1.0, base=0,
                               pattern=[[-1, P]], channel_multiplier=1).then_inc(s_.const, 1)
            pool.affine_select(out=FLIP[:], in_=FLIP[:], compare_op=ALU.not_equal, fill=1.0, base=1 - P,
                               pattern=[[1, P]], channel_multiplier=1).then_inc(s_.flip_ready, 1)
            pool.wait_ge(s_.tab_in, 16)
            pool.tensor_copy(EXT[:, 0:127], EXT[:, 127:128].to_broadcast([16, 127])).then_inc(s_.ext_ready, 1)
            pool.wait_ge(s_.vec_in, 16)
            pool.wait_ge(s_.row_in, 48)
            fg, g3 = vec_at["final_norm_g"], vec_at["mix_norm_g_2"]
            pc(pool.memset(W2[:, :, 0:1], 1.0))
            pc(pool.tensor_tensor(W2[:, :, 1], VEC[:, fg:fg + KB], VEC[:, fg:fg + KB], ALU.mult))
            pc(pool.tensor_tensor(G23[:], VEC[:, fg:fg + KB], VEC[:, g3:g3 + KB], ALU.mult))
            pc.wait(pool)
            pool.tensor_tensor(WBA[:], WBA[:], G23[:, :, None].to_broadcast([P, KB, 16]), ALU.mult).then_inc(s_.prep, 1)
            norm_add(pool, pc, 0)
            iot = nc.alloc_sbuf_tensor_at("IOT", [P, TOK], mybir.dt.int32, offset=base + int((Z + 89) * K1))
            pc(pool.iota(iot[:], pattern=[[1, TOK]], base=-P, channel_multiplier=-1))
            pc.wait(pool)
            pc(pool.tensor_copy(NALI[:], iot[:]))
            pc.wait(pool)
            pool.affine_select(out=NALI[:], in_=NALI[:], compare_op=ALU.is_ge, fill=NEG, base=P,
                               pattern=[[-1, TOK]], channel_multiplier=1).then_inc(s_.const, 1)
            pool.wait_ge(s_.bias_in, 16)
            pool.wait_ge(s_.const, 3)
            pool.memset(BREV[64:P, :, 192:TOK], NEG).then_inc(s_.bias_masked, 1)

            for j in range(KB):
                if j % 2 == 0:
                    c = seg["xg"].first + j // 2
                    pool.wait_ge(freed[c % SLOTS], c // SLOTS + 1)
                pc(pool.tensor_scalar(XN[:, j], XR[:, j, 0:TOK], vec("conv_w", j), vec("conv_b", j), ALU.mult, ALU.add))
                for t in range(1, 4):
                    pc.wait(pool)
                    pc(pool.tensor_scalar(TAP[:, 0], XR[:, j, t:t + TOK], vec("conv_w", 8 * t + j), 1.0, ALU.mult, ALU.mult))
                    pc.wait(pool)
                    ins = pool.tensor_tensor(XN[:, j], XN[:, j], TAP[:, 0], ALU.add)
                    if t < 3:
                        pc(ins)
                    else:
                        ins.then_inc(s_.conv_done, 1)
                        pool.wait_ge(s_.conv_done, j + 1)

            for h in range(2):
                for j in range(4 * h, 4 * h + 4):
                    pool.wait_ge(s_.gates_done, 2 * j + 2)
                    pc(pool.tensor_tensor(RI[:, j], RI[:, j], XN[:, j], ALU.mult))
                pc.wait(pool)
                pool.wait_ge(s_.rt_done, h + 1)
                hb = slice(4 * h, 4 * h + 4)
                pool.tensor_tensor(RI[:, hb], RI[:, hb], MU[:, hb], ALU.mult).then_inc(s_.ri_done, 1)
            pool.wait_ge(s_.gl_done, 1)
            for p in range(4):
                pool.wait_ge(s_.scanned, 2 * p + 2)
                blk = slice(2 * p, 2 * p + 2)
                pool.tensor_tensor(XN[:, blk], XN[:, blk], GR[:, blk], ALU.mult).then_inc(s_.hs_ready, 1)
            pc(pool.memset(TRI[:], 1.0))
            pc(pool.memset(NEGL[:], 0.0))
            pc(pool.memset(NEGU[:], 0.0))
            pc(pool.memset(LM[:], 1.0))
            pc.wait(pool)
            pc(pool.affine_select(out=TRI[:], in_=TRI[:], compare_op=ALU.is_ge, fill=0.0, base=0,
                                  pattern=[[1, P]], channel_multiplier=-1))
            pc(pool.affine_select(out=NEGL[:], in_=NEGL[:], compare_op=ALU.is_gt, fill=NEG, base=0,
                                  pattern=[[-1, P]], channel_multiplier=1))
            pc(pool.affine_select(out=NEGU[:], in_=NEGU[:], compare_op=ALU.is_ge, fill=NEG, base=0,
                                  pattern=[[1, P]], channel_multiplier=-1))
            for l in range(7):
                w = 1 << l
                m = LM[:, l].rearrange("p (b two c) -> p b two c", two=2, c=w)
                pc(pool.memset(m[:, :, 1, :], 0.0))
                pc.wait(pool)
                pc(pool.affine_select(out=m[:, :, 0, :], in_=m[:, :, 0, :], compare_op=ALU.is_ge, fill=0.0, base=-w,
                                      pattern=[[-2 * w, P // (2 * w)], [0, w]], channel_multiplier=1))
                pc.wait(pool)
                pc(pool.affine_select(out=m[:, :, 0, :], in_=m[:, :, 0, :], compare_op=ALU.is_ge, fill=0.0, base=2 * w - 1,
                                      pattern=[[2 * w, P // (2 * w)], [0, w]], channel_multiplier=-1))
            norm_add(pool, pc, 1)
            add_rows(pool, seg["fo"])
            pool.wait_ge(mm_done, seg["fo"].first + seg["fo"].n)
            pc.wait(pool)
            pool.memset(UQ[:, :, 0:3], 0.0).then_inc(s_.uq_zero, 1)

            def last_tap(st):
                w = VEC[:, bass.ds(st.rel_at(-1) * 2 + vec_at["dn_conv_w_2"] + 72, 2), None].to_broadcast([P, 2, TOK])
                y = QKV[:, bass.ds(st.rel_at(-1) * 2, 2), :]
                pool.wait_ge(freed[slot_of(st, -1)], st.uses(-1))
                if st.i is not None or st.j > 1:
                    pool.wait_ge(s_.tapped, st.local(-2))
                pool.tensor_tensor(TAP2[:], UQ[:, bass.ds(st.rel_at(-1) * 2, 2), 3:TOK + 3], w, ALU.mult).then_inc(s_.tap3, 1)
                pool.wait_ge(s_.tap2, st.local(-2, 2))
                pool.wait_ge(s_.tap3, st.local(-1))
                pool.tensor_tensor(y, y, TAP2[:], ALU.add).then_inc(s_.tapped, 1)
            steps(pool, seg["dq"], lambda st: last_tap(st) if st.i is not None or st.j else None, head=3, tail=3)
            last_tap(Step(seg["dq"], seg["dq"].n, None))

            for g in range(4):
                am = AM[:, 4 * g:4 * g + 4]
                pool.wait_ge(s_.d_done, 2 * g + 1)
                pool.tensor_tensor(am, am, BETA[:, 4 * g:4 * g + 4, None].to_broadcast([P, 4, P]), ALU.mult).then_inc(s_.ab_done, 1)
            pool.wait_ge(s_.rh_ready, 1)
            pool.wait_ge(s_.xl_ready, 12)
            pool.wait_ge(s_.ba_done, 1)
            pc(pool.tensor_tensor(H[:], H[:], RH[:, None, :].to_broadcast([P, KB, TOK]), ALU.mult))
            pc.wait(pool)
            pool.tensor_tensor(H[:], H[:], VEC[:, fg:fg + KB, None].to_broadcast([P, KB, TOK]), ALU.mult).then_inc(s_.h2, 1)

            for l in range(7):
                for g in range(4):
                    n = 4 * l + g
                    if l == 0:
                        pool.wait_ge(s_.a_done, g + 1)
                    if l == 1:
                        pool.wait_ge(s_.tx_in, g + 1)
                        pool.wait_ge(s_.ty_out, g + 1)
                    elif l > 1:
                        pool.wait_ge(s_.p1_done, n - 7)
                    pool.tensor_tensor(CM[:, 4 * g:4 * g + 4], AM[:, 4 * g:4 * g + 4],
                                       LM[:, l, None, :].to_broadcast([P, 4, P]), ALU.mult).then_inc(s_.c_done, 1)
            pool.wait_ge(s_.zs_done, 4)
            pool.tensor_scalar(ZS[:], ZS[:], vec("dn_out_norm_g_2", 0), 1.0, ALU.mult, ALU.mult).then_inc(s_.zg_done, 1)
            norm_add(pool, pc, 3)
            add_rows(pool, seg["w0"])
            norm_add(pool, pc, 4)
            norm_add(pool, pc, 5)
            add_rows(pool, seg["w1"])

        def hidden_hi(act, st, width):
            k = slot_of(st, -1)
            act.activation(hid(HH, st, width), HP[:, k, 0:width * TOK].rearrange("p (c t) -> p c t", c=width),
                           ACT.Copy).then_inc(s_.hh_done, 1)

        def hid(t, st, width):
            return t[:, bass.ds(st.rel_at(-1) * width, width), :]

        def hidden_lo(dve, st, width, earlier):
            k = slot_of(st, -1)
            dve.wait_ge(s_.hh_done, st.local(earlier - 1))
            dve.tensor_tensor(hid(HL, st, width), HP[:, k, 0:width * TOK].rearrange("p (c t) -> p c t", c=width),
                              hid(HH, st, width).bitcast(F32), ALU.subtract).then_inc(s_.hl_done, 1)

        HBASE = {"fi": 0, "u0": 22, "u1": 38}

        def silu_ready(act, st):
            act.wait_ge(freed[slot_of(st, -1)], st.uses(-1))

        def squares_ready(earlier):
            def ready(act, st):
                act.wait_ge(s_.hp_done, st.local(earlier - 1))
            return ready

        @block.scalar
        def _(act):
            act.dma_start(VEC[:], a["vectors"]).then_inc(s_.vec_in, 16)
            act.dma_start(EXT[:, 127:384], a["rel_reversed"]).then_inc(s_.tab_in, 16)
            act.dma_start(AROW[:], a["dn_a_log"].partition_broadcast(P)).then_inc(s_.row_in, 16)
            act.dma_start(DTB[:], a["dn_dt_bias"].partition_broadcast(P)).then_inc(s_.row_in, 16)
            act.dma_start(WBA[:], cols(a["dn_w_in"], 4096, 16)).then_inc(s_.row_in, 16)
            act.wait_ge(s_.vec_in, 16)
            first = Step(seg["qk"], 0, None)
            for p in range(4):
                norm_high(act, 0, p, squares=False)
            split_hi(act, first, 0)
            for p in range(4):
                squares(act, 0, p)
            split_hi(act, first, 1)
            act.wait_ge(s_.wri_zero, 1)
            act.wait_ge(s_.pool, 2)
            for r, w in enumerate(("w_rg_r", "w_rg_i")):
                for e in range(2):
                    act.dma_start(WRI[64 * e:64 * e + 64, r, :, 64 * e:64 * e + 64],
                                  a[w].rearrange("(j e) d f -> e d j f", e=2)[e]).then_inc(s_.wri_in, 16)
            act.wait_ge(s_.ext_ready, 1)
            act.dma_start(ext_dram, EXT[:]).then_inc(s_.ext_out, 16)
            act.wait_ge(s_.ext_out, 16)
            act.dma_start(BREV[:], bass.AP(tensor=ext_dram.tensor, offset=0, ap=[[1, P], [384, 16], [1, TOK]])).then_inc(s_.bias_in, 16)

            def qk(st):
                split_hi(act, st)
                if st.i is None and st.j == 0:
                    act.wait_ge(s_.const, 1)
                    norm_root(act, 0)
                if st.i is None and st.j == 2:
                    act.wait_ge(s_.ey_done, 1)
                    act.activation(SMALL[:, 1, 0:8], SMALL[:, 1, 0:8], ACT.Exp, scale=-1.0).then_inc(s_.sm_ready, 1)
                    for n in range(8):
                        act.wait_ge(s_.bias_turned, n + 1)
                        act.activation(BIAS[:, 2 * n:2 * n + 2], two(PS[:, 6 + n % 2, :]), ACT.Copy).then_inc(s_.bias_ready, 1)
            steps(act, seg["qk"], qk, head=SLOTS)
            steps(act, seg["v"], lambda st: split_hi(act, st))

            for st in (Step(seg["xg"], j, None) for j in range(8)):
                split_hi(act, st)
                attn_exp(act, st.j)
                if st.j:
                    attn_oh(act, st.j - 1)
                attn_pt(act, st.j)

            def sigmoid(out, ps, bias):
                return act.activation(out, ps, ACT.Sigmoid, bias=bias)

            def decay(j):
                act.wait_ge(s_.gates_done, 2 * j + 1)
                act.activation(RR[:, j], RR[:, j], ACT.Exp, scale=NSP8[:, j:j + 1]).then_inc(s_.ea_done, 1)

            def root(h):
                act.wait_ge(s_.mu_ready, h + 1)
                act.activation(MU[:, 4 * h:4 * h + 4], MU[:, 4 * h:4 * h + 4], ACT.Sqrt).then_inc(s_.rt_done, 1)

            for st in (Step(seg["gab"], j, None) for j in range(8)):
                j = st.j
                split_hi(act, st)
                if j == 0:
                    attn_oh(act, 7)
                    act.activation(GR[:], GR[:], ACT.Gelu_apprx_tanh).then_inc(s_.gl_done, 1)
                if j == 5:
                    for b in range(4):
                        decay(b)
                act.wait_ge(s_.rg_done, j + 1)
                sigmoid(RR[:, j], PS[:, 3 + j % 2, 0:TOK], vec("b_rg_r", j)).then_inc(s_.gates_done, 1)
                sigmoid(RI[:, j], PS[:, 3 + j % 2, TOK:512], vec("b_rg_i", j)).then_inc(s_.gates_done, 1)
                act.wait_ge(freed[st.slot], st.uses())
                sigmoid(GAB[:, 2 * j], GAB[:, 2 * j], vec("b_merge", 2 * j))
                sigmoid(GAB[:, 2 * j + 1], GAB[:, 2 * j + 1], vec("b_merge", 2 * j + 1)).then_inc(s_.gab_done, 1)
                act.wait_ge(s_.gates_done, 2 * j + 1)
                act.activation(TH[:, j], RR[:, j], ACT.Tanh, scale=SP8[:, j:j + 1]).then_inc(s_.th_done, 1)

            for st in (Step(seg["ao"], j, None) for j in range(4)):
                split_hi(act, st)
                if st.j == 0:
                    for b in range(4, 8):
                        decay(b)
                    root(0)
                    root(1)
            for p in range(4):
                act.wait_ge(s_.hs_ready, p + 1)
                act.activation(XH[:, 2 * p:2 * p + 2], XN[:, 2 * p:2 * p + 2], ACT.Copy).then_inc(s_.yh_done, 1)

            def mix_high(p):
                act.wait_ge(s_.mix_ready, p + 1)
                act.activation(OH[:, 2 * p:2 * p + 2], MIX[:, 2 * p:2 * p + 2], ACT.Copy).then_inc(s_.mh_done, 1)

            for st in (Step(seg["ro"], j, None) for j in range(4)):
                split_hi(act, st)
                if st.j:
                    mix_high(st.j - 1)
            mix_high(3)

            def residual(name, m):
                for st in (Step(seg[name], j, None) for j in range(4)):
                    split_hi(act, st)
                    if st.j:
                        norm_high(act, m, st.j - 1)
                norm_high(act, m, 3)

            residual("wo", 1)

            def gate(st):
                last = st.i is None and st.j == st.seg.n - 1
                if not last:
                    split_hi(act, st)
                if st.i is None and st.j == 0:
                    norm_root(act, 1)
                if st.i is not None or st.j:
                    silu_ready(act, st)
                act.wait_ge(s_.sg_in, st.local())
                act.activation(SG[:, st.slot, 0:TOK], SG[:, st.slot, 0:TOK], ACT.Silu).then_inc(s_.sg_done, 1)
                if st.i is not None or st.j:
                    hidden_hi(act, st, 1)
            steps(act, seg["fi"], gate, head=1, tail=1)
            end = Step(seg["fi"], seg["fi"].n, None)
            split_hi(act, Step(seg["fi"], seg["fi"].n - 1, None))
            silu_ready(act, end)
            hidden_hi(act, end, 1)
            def row_chunks(w, m):
                steps(act, w, lambda st: split_hi(act, st) if st.i is not None or st.j < w.n - 1 else None, tail=SLOTS - 1)
                for p in range(4):
                    norm_high(act, m, p)
                split_hi(act, Step(w, w.n - 1, None))

            act.wait_ge(s_.prep, 1)
            row_chunks(seg["fo"], 2)

            def tap0(st):
                for b in range(2):
                    blk = st.rel_at(-1) * 2 + b
                    act.activation(QKV[:, bass.ds(blk, 1), :], UQ[:, bass.ds(blk, 1), 0:TOK], ACT.Copy,
                                   scale=vec("dn_conv_w_2", blk)).then_inc(s_.tap0, 1)

            def silu(st):
                blk = QKV[:, bass.ds(st.rel_at(-3) * 2, 2), :]
                act.activation(blk, blk, ACT.Silu).then_inc(s_.silu_done, 1)

            def dq(st):
                if st.i is not None or st.j >= 1:
                    act.wait_ge(freed[slot_of(st, -1)], st.uses(-1))
                if st.i is not None or st.j >= 3:
                    act.wait_ge(s_.tapped, st.local(-3))
                split_hi(act, st)
                if st.i is None and st.j == 0:
                    norm_root(act, 2)
                if st.i is None and st.j == 1:
                    act.wait_ge(s_.ba_done, 1)
                    for c in range(TT):
                        act.activation(BETA[:, 8 * c:8 * c + 8], PS[:, 3, 256 + 16 * c:264 + 16 * c], ACT.Sigmoid,
                                       scale=RC[:, c:c + 1]).then_inc(s_.beta_done, 1)
                    act.wait_ge(s_.ey_done, 2)
                    act.activation(SMALL[:, 1], SMALL[:, 1], ACT.Exp, scale=-1.0).then_inc(s_.sm_ready, 1)
                    act.activation(AROW[:], AROW[:], ACT.Exp).then_inc(s_.sm_ready, 1)
                if st.i is None and st.j == 2:
                    act.wait_ge(s_.gc_done, 1)
                    act.activation(EGC[:], GC[:], ACT.Exp).then_inc(s_.sm_ready, 1)
                if st.i is not None or st.j >= 1:
                    tap0(st)
                if st.i is not None or st.j >= 3:
                    silu(st)
            steps(act, seg["dq"], dq, head=3, tail=3)
            for st in (Step(seg["dz"], j, None) for j in range(4)):
                q = Step(seg["dq"], seg["dq"].n + st.j, None)
                if st.j == 0:
                    act.wait_ge(freed[slot_of(q, -1)], q.uses(-1))
                    tap0(q)
                split_hi(act, st)
                if st.j == 0:
                    act.activation(SQK[:], QKV[:, 8:16], ACT.Square).then_inc(s_.l2sq, 1)
                if st.j == 1:
                    act.activation(XN[:], QKV[:, 0:8], ACT.Square).then_inc(s_.l2sq, 1)
                if st.j <= 2:
                    act.wait_ge(s_.tapped, q.local(-3))
                    silu(q)
                if st.j >= 2:
                    for g in (2 * st.j - 4, 2 * st.j - 3):
                        for t, d in enumerate((AM, AT)):
                            act.wait_ge(s_.dt_ready, 2 * g + t + 1)
                            act.activation(d[:, 4 * g:4 * g + 4], d[:, 4 * g:4 * g + 4], ACT.Exp).then_inc(s_.d_done, 1)
            for u in range(2):
                act.wait_ge(s_.l2sum, u + 1)
                act.activation(RNS[:, 16 * u:16 * u + 16], PS[:, 4 + u, 0:16], ACT.Sqrt, bias=EPSC[:]).then_inc(s_.l2sd, 1)
            for j in range(4):
                zs = ZS[:, 2 * j:2 * j + 2]
                st = Step(seg["dz"], j, None)
                act.wait_ge(freed[st.slot], st.uses())
                act.activation(zs, zs, ACT.Silu).then_inc(s_.zs_done, 1)
            def copy_x(n):
                g = n % 4
                act.wait_ge(s_.x_done, n + 1)
                act.activation(TX[:, 4 * g:4 * g + 4], PS[:, 2 + n % 2, :].rearrange("p (n i) -> p n i", n=4), ACT.Copy).then_inc(s_.x_out, 1)
            for n in range(24):
                g = n % 4
                act.wait_ge(s_.p1_done, n + 1)
                act.activation(P1[:, 4 * g:4 * g + 4], PS[:, n % 2, :].rearrange("p (n i) -> p n i", n=4), ACT.Copy).then_inc(s_.p1_out, 1)
                if 2 <= n < 22:
                    copy_x(n - 2)
            for g in range(2):
                act.wait_ge(s_.w_done, g + 1)
                act.activation(NW[:, 4 * g:4 * g + 4], PS[:, g, :].rearrange("p (n i) -> p n i", n=4), ACT.Copy, scale=-1.0).then_inc(s_.w_out, 1)
            for u in range(4):
                act.wait_ge(s_.o_out, u + 1)
                act.activation(OSQ[:, 2 * u:2 * u + 2], OD[:, 2 * u:2 * u + 2], ACT.Square).then_inc(s_.osq, 1)
            act.wait_ge(s_.osum, 1)
            act.activation(RNS[:, 0:16], PS[:, 4, 0:16], ACT.Sqrt, bias=EPSC[:], scale=1.0 / P).then_inc(s_.osd, 1)
            for u in range(4):
                act.wait_ge(s_.on2, u + 1)
                act.activation(DOH[:, 2 * u:2 * u + 2], OD[:, 2 * u:2 * u + 2], ACT.Copy).then_inc(s_.oo, 1)
            residual("do", 3)

            def mlp(layer):
                sq = squares_ready(16 * layer)

                def up(st):
                    split_hi(act, st)
                    if st.i is None and st.j == 1:
                        norm_root(act, 3 + 2 * layer)
                    act.wait_ge(mm_done, st.count())
                    if st.i is not None or st.j:
                        sq(act, st)
                    act.activation(SG[:, st.slot, :], PS[:, st.slot, :], ACT.Relu).then_inc(freed[st.slot], 1)
                    if st.i is not None or st.j:
                        hidden_hi(act, st, 2)
                u = seg[f"u{layer}"]
                steps(act, u, up, head=2)
                end = Step(u, u.n, None)
                sq(act, end)
                hidden_hi(act, end, 2)
                w = seg[f"w{layer}"]
                row_chunks(w, 4 + 2 * layer)

            mlp(0)

            for t in range(12):
                split_hi(act, moba_step(t))
                if t == 0:
                    norm_root(act, 4)
                if 3 <= t <= 9 and t % 2:
                    attn_exp(act, 8 + (t - 3) // 2)
                    attn_pt(act, 8 + (t - 3) // 2)
                if t >= 10:
                    attn_oh(act, 8 + t - 10)
            attn_oh(act, 10)
            attn_oh(act, 11)
            residual("mo", 5)
            mlp(1)
            norm_root(act, FINAL)

        @block.vector
        def _(dve):
            ch = Chain(s_.dve)

            def softplus(n, ready):
                v = [SMALL[:, i, 0:n] for i in range(6)]
                ch.wait(dve)
                dve.scalar_tensor_tensor(out=v[1], in0=v[0], scalar=-1.0, in1=v[0], op0=ALU.mult, op1=ALU.max).then_inc(s_.ey_done, 1)
                dve.wait_ge(s_.sm_ready, ready)
                ch(dve.tensor_scalar(v[2], v[1], 2.0, None, ALU.add))
                ch.wait(dve)
                ch(dve.reciprocal(v[2], v[2]))
                ch.wait(dve)
                ch(dve.tensor_tensor(v[2], v[2], v[1], ALU.mult))
                ch.wait(dve)
                ch(dve.tensor_tensor(v[3], v[2], v[2], ALU.mult))
                ch.wait(dve)
                ch(dve.tensor_scalar(v[4], v[3], 1.0 / 17, None, ALU.mult))
                for k in range(7, 0, -1):
                    ch.wait(dve)
                    ch(dve.scalar_tensor_tensor(out=v[4], in0=v[4], scalar=1.0 / (2 * k + 1), in1=v[3], op0=ALU.add, op1=ALU.mult))
                ch.wait(dve)
                ch(dve.scalar_tensor_tensor(out=v[4], in0=v[4], scalar=1.0, in1=v[2], op0=ALU.add, op1=ALU.mult))
                ch(dve.tensor_scalar(v[5], v[0], 0.0, None, ALU.max))
                ch.wait(dve)
                ch(dve.scalar_tensor_tensor(out=v[5], in0=v[4], scalar=2.0, in1=v[5], op0=ALU.mult, op1=ALU.add))
                ch.wait(dve)
                return v[5]

            def read_out(st, out, by=None):
                dve.wait_ge(mm_done, st.count())
                dve.tensor_tensor(out, bank(st), by_rows(2) if by is None else by, ALU.mult).then_inc(freed[st.slot], 1)

            dve.wait_ge(s_.vec_in, 16)
            first = Step(seg["qk"], 0, None)
            for p in range(4):
                norm_low(dve, 0, p)
            split_lo(dve, first, 0)
            split_lo(dve, first, 1)

            def qk(st):
                split_lo(dve, st)
                if st.i is None and st.j == 0:
                    norm_scale(dve, ch, 0)
                read_out(st, QK[:, bass.ds(st.rel * 2, 2), :])
                if st.i is None and st.j == 1:
                    lam = vec_at["rg_lambda"]
                    ch(dve.tensor_scalar(SMALL[:, 0, 0:8], VEC[:, lam:lam + 8], -1.0, None, ALU.mult))
                    sp = softplus(8, 1)
                    ch(dve.tensor_scalar(SP8[:], sp, 8.0, None, ALU.mult))
                    ch(dve.tensor_scalar(NSP8[:], sp, -8.0, None, ALU.mult))
            steps(dve, seg["qk"], qk, head=SLOTS)

            def read_v(st):
                read_out(st, VT[:, :, bass.ds(st.rel * NCOL, NCOL)], RC[:, 0:2, None].to_broadcast([P, TT, NCOL]))

            def v(st):
                split_lo(dve, st)
                read_v(st)
            steps(dve, seg["v"], v)

            dve.wait_ge(s_.bias_ready, 8)
            for st in (Step(seg["xg"], j, None) for j in range(8)):
                j = st.j
                attn_shift(dve, ch, j)
                split_lo(dve, st)
                attn_scale(dve, ch, j)
                read_out(st, XR[:, 2 * j:2 * j + 2, 3:TOK + 3] if j < 4 else GR[:, 2 * j - 8:2 * j - 6])
                if j:
                    attn_ol(dve, j - 1)

            def one_less_square(h):
                hb = slice(4 * h, 4 * h + 4)
                dve.wait_ge(s_.ea_done, 4 * h + 4)
                dve.wait_ge(s_.th_done, 4 * h + 4)
                ch(dve.tensor_tensor(MU[:, hb], RR[:, hb], RR[:, hb], ALU.mult))
                ch.wait(dve)
                dve.scalar_tensor_tensor(out=MU[:, hb], in0=MU[:, hb], scalar=1.0, in1=TH[:, hb], op0=ALU.add,
                                         op1=ALU.mult).then_inc(s_.mu_ready, 1)

            def scan(h):
                dve.wait_ge(s_.ri_done, h + 1)
                for b in range(4 * h, 4 * h + 4):
                    dve.tensor_tensor_scan(XN[:, b], RR[:, b], RI[:, b], 0.0, ALU.mult, ALU.add).then_inc(s_.scanned, 1)

            for st in (Step(seg["gab"], j, None) for j in range(8)):
                split_lo(dve, st)
                if st.j == 0:
                    attn_ol(dve, 7)
                dve.wait_ge(mm_done, st.count())
                dve.tensor_tensor(GAB[:, 2 * st.j:2 * st.j + 2], bank(st), by_rows(2), ALU.mult).then_inc(freed[st.slot], 1)
                if st.j == 5:
                    one_less_square(0)

            for st in (Step(seg["ao"], j, None) for j in range(4)):
                j = st.j
                split_lo(dve, st)
                dve.wait_ge(mm_done, st.count())
                dve.wait_ge(s_.gab_done, 8)
                dve.tensor_tensor(MIX[:, 2 * j:2 * j + 2], bank(st), GAB[:, 2 * j:2 * j + 2], ALU.mult).then_inc(freed[st.slot], 1)
                if j == 0:
                    one_less_square(1)
                if j == 1:
                    scan(0)
                    scan(1)
            for p in range(4):
                blk = slice(2 * p, 2 * p + 2)
                dve.wait_ge(s_.yh_done, p + 1)
                dve.tensor_tensor(XL[:, blk], XN[:, blk], XH[:, blk].bitcast(F32), ALU.subtract).then_inc(s_.y_done, 1)

            def mix_lo(p):
                blk = slice(2 * p, 2 * p + 2)
                dve.wait_ge(s_.mh_done, p + 1)
                dve.tensor_tensor(OL[:, blk], MIX[:, blk], OH[:, blk].bitcast(F32), ALU.subtract).then_inc(s_.ml_done, 1)

            for st in (Step(seg["ro"], j, None) for j in range(4)):
                blk = slice(2 * st.j, 2 * st.j + 2)
                split_lo(dve, st)
                if st.j:
                    mix_lo(st.j - 1)
                dve.wait_ge(mm_done, st.count())
                dve.tensor_tensor(MU[:, blk], bank(st), GAB[:, 8 + 2 * st.j:10 + 2 * st.j], ALU.mult).then_inc(freed[st.slot], 1)
                dve.wait_ge(freed[st.slot], st.base // SLOTS + 1)
                dve.tensor_tensor(MIX[:, blk], MIX[:, blk], MU[:, blk], ALU.add).then_inc(s_.mix_ready, 1)
            mix_lo(3)

            def residual(name, m):
                for st in (Step(seg[name], j, None) for j in range(4)):
                    split_lo(dve, st)
                    if st.j:
                        norm_low(dve, m, st.j - 1)
                    hb = H[:, 2 * st.j:2 * st.j + 2]
                    dve.wait_ge(mm_done, st.count())
                    dve.tensor_tensor(hb, hb, bank(st), ALU.add).then_inc(freed[st.slot], 1)
                norm_low(dve, m, 3)

            def row_chunks(w, m):
                steps(dve, w, lambda st: split_lo(dve, st) if st.i is not None or st.j < w.n - 1 else None, tail=SLOTS - 1)
                scale_rows(dve, w, m)
                split_lo(dve, Step(w, w.n - 1, None))

            residual("wo", 1)

            def up(st):
                last = st.i is None and st.j == st.seg.n - 1
                if not last:
                    split_lo(dve, st)
                if st.i is None and st.j == 0:
                    norm_scale(dve, ch, 1)
                dve.wait_ge(mm_done, st.count())
                dve.tensor_tensor(SG[:, st.slot, 0:TOK], PS[:, st.slot, 0:TOK], RSTD[:], ALU.mult).then_inc(s_.sg_in, 1)
                dve.wait_ge(s_.sg_done, st.local())
                dve.tensor_tensor(HP[:, st.slot, 0:TOK], PS[:, st.slot, TOK:512], SG[:, st.slot, 0:TOK], ALU.mult).then_inc(freed[st.slot], 1)
                if st.i is not None or st.j:
                    hidden_lo(dve, st, 1, 0)
            steps(dve, seg["fi"], up, head=1, tail=1)
            split_lo(dve, Step(seg["fi"], seg["fi"].n - 1, None))
            hidden_lo(dve, Step(seg["fi"], seg["fi"].n, None), 1, 0)
            row_chunks(seg["fo"], 2)

            def taps(st):
                for t in range(2):
                    for b in range(2):
                        blk = st.rel_at(-1) * 2 + b
                        if t == 0:
                            dve.wait_ge(s_.tap0, st.local(b - 3, 2))
                        else:
                            dve.wait_ge(s_.tap1, st.local(b - 3, 2))
                        y = QKV[:, bass.ds(blk, 1), :]
                        dve.scalar_tensor_tensor(out=y, in0=UQ[:, bass.ds(blk, 1), t + 1:t + 1 + TOK],
                                                 scalar=vec("dn_conv_w_2", blk + 24 * (t + 1)), in1=y,
                                                 op0=ALU.mult, op1=ALU.add).then_inc((s_.tap1, s_.tap2)[t], 1)

            def per_head(t):
                return t[:, :, None].to_broadcast([P, 4, P])

            def dq(st):
                split_lo(dve, st)
                if st.i is None and st.j == 0:
                    norm_scale(dve, ch, 2)
                if st.i is None and st.j == 1:
                    dve.wait_ge(s_.beta_done, 2)
                    for c in range(TT):
                        ch(dve.scalar_tensor_tensor(out=SMALL[:, 0, 8 * c:8 * c + 8], in0=PS[:, 3, 264 + 16 * c:272 + 16 * c],
                                                    scalar=RC[:, c:c + 1], in1=DTB[:], op0=ALU.mult, op1=ALU.add))
                    sp = softplus(16, 3)
                    ch(dve.tensor_tensor(GT[:].rearrange("p (c h) -> p c h", c=TT), sp.rearrange("p (c h) -> p c h", c=TT),
                                         AROW[:, None, :].to_broadcast([P, TT, 8]), ALU.mult))
                    ch.wait(dve)
                    dve.tensor_scalar(GT[:], GT[:], -1.0, None, ALU.mult).then_inc(s_.g_ready, 1)
                if st.i is None and st.j == 2:
                    dve.wait_ge(s_.gc_sum, 1)
                    dve.tensor_copy(GC[:], PS[:, 3, 320:336]).then_inc(s_.gc_done, 1)
                    dve.wait_ge(s_.sm_ready, 4)
                    ch(dve.tensor_tensor(BEG[:], BETA[:, 8:16], EGC[:, 8:16], ALU.mult))
                if st.i is None and st.j == 0:
                    dve.wait_ge(s_.uq_zero, 1)
                read_out(st, UQ[:, bass.ds(st.rel * 2, 2), 3:TOK + 3])
                if st.i is not None or st.j:
                    taps(st)
                if st.i is None and st.j >= 9:
                    exponents(st.j - 9)

            def four(b):
                return PS[:, b, :].rearrange("p (n i) -> p n i", n=4)

            def exponents(g):
                r = slice(4 * g, 4 * g + 4)
                dve.wait_ge(s_.b_done, g + 1)
                ch(dve.tensor_tensor(AM[:, r], NEGL[:, None, :].to_broadcast([P, 4, P]), four(6 + g % 2), ALU.subtract))
                dve.tensor_tensor(AT[:, r], NEGU[:, None, :].to_broadcast([P, 4, P]), four(6 + g % 2), ALU.add).then_inc(s_.b_read, 1)
                ch.wait(dve, ch.n)
                dve.tensor_tensor(AM[:, r], AM[:, r], per_head(GC[:, r]), ALU.add).then_inc(s_.dt_ready, 1)
                dve.wait_ge(s_.b_read, g + 1)
                dve.tensor_tensor(AT[:, r], AT[:, r], per_head(GC[:, r]), ALU.subtract).then_inc(s_.dt_ready, 1)

            steps(dve, seg["dq"], dq, head=3, tail=3)
            for st in (Step(seg["dz"], j, None) for j in range(4)):
                split_lo(dve, st)
                if st.j == 0:
                    taps(Step(seg["dq"], seg["dq"].n, None))
                dve.wait_ge(mm_done, st.count())
                dve.tensor_tensor(ZS[:, 2 * st.j:2 * st.j + 2], bank(st), by_rows(2), ALU.mult).then_inc(freed[st.slot], 1)
                if st.j == 0:
                    exponents(3)

            for u in range(2):
                dve.wait_ge(s_.l2sd, u + 1)
                dve.reciprocal(RNC[:, 16 * u:16 * u + 16], RNS[:, 16 * u:16 * u + 16]).then_inc(s_.rnc, 1)

            def systems(block_, g):
                b = block_ + 4 * (g % 2)
                return QKV[:, b:b + 4, (g // 2) * P:(g // 2) * P + P]

            for u in range(8):
                dve.wait_ge(s_.unit_rows, u + 1)
                t = systems(8 if u < 4 else 0, u % 4)
                dve.scalar_tensor_tensor(out=t, in0=t, scalar=1.0 if u < 4 else P ** -0.5, in1=four(UB[u]), op0=ALU.mult,
                                         op1=ALU.mult).then_inc(s_.l2done, 1)
            for g in range(4):
                r = slice(4 * g, 4 * g + 4)
                dve.wait_ge(s_.gk_done, g + 1)
                dve.wait_ge(s_.ab_done, g + 1)
                dve.tensor_tensor(AM[:, r], AM[:, r], four(UB[g]), ALU.mult).then_inc(s_.a_done, 1)
            def attention(g):
                r = slice(4 * g, 4 * g + 4)
                dve.wait_ge(s_.d_done, 2 * g + 2)
                if g < 2:
                    ch(dve.tensor_copy(LAST[:, r], AT[:, r, P - 1:P].rearrange("p n i -> p (n i)")))
                    ch.wait(dve)
                dve.wait_ge(s_.kq_done, g + 1)
                dve.tensor_tensor(AT[:, r], AT[:, r], four(UB[4 + g]), ALU.mult).then_inc(s_.at_done, 1)
            ident4 = IDENT[:, None, :].to_broadcast([P, 4, P])
            attention(0)
            attention(1)
            for g in range(4):
                r = slice(4 * g, 4 * g + 4)
                if g in (1, 2):
                    attention(g + 1)
                dve.wait_ge(s_.c_done, g + 1)
                dve.tensor_tensor(TX[:, r], ident4, CM[:, r], ALU.subtract).then_inc(s_.tx_in, 1)
                dve.wait_ge(s_.ct_done, g + 1)
                dve.tensor_tensor(TY[:, r], ident4, four(UB[g]), ALU.subtract).then_inc(s_.ty_out, 1)
            for n in range(24):
                r = slice(4 * (n % 4), 4 * (n % 4) + 4)
                dve.wait_ge(s_.q_done, n + 1)
                dve.tensor_tensor(TY[:, r], TY[:, r], four(4 + n % 2), ALU.subtract).then_inc(s_.ty_out, 1)
                if n < 10:
                    dve.wait_ge(s_.tr_done, n + 1)
                if n < 8:
                    out, by = (VB[:, r], BETA[:, r]) if n < 4 else (KD[:, r], LAST[:, r]) if n < 6 else \
                        (KBT[:, 4 * (n - 6):4 * (n - 6) + 4], BEG[:, 4 * (n - 6):4 * (n - 6) + 4])
                    dve.tensor_tensor(out, four(6 + n % 2), per_head(by), ALU.mult).then_inc(s_.vt_out, 1)
                elif n < 10:
                    q = systems(0, n - 6)
                    dve.tensor_tensor(q, q, four(6 + n % 2), ALU.mult).then_inc(s_.vt_out, 1)
            for g in range(2):
                dve.wait_ge(s_.vn0, g + 1)
                dve.tensor_copy(VN[:, 4 * g:4 * g + 4], four(6 + g)).then_inc(s_.vn0_out, 1)
            for g in range(2):
                dve.wait_ge(s_.s_done, g + 1)
                dve.tensor_copy(ST[:, 4 * g:4 * g + 4], four(2 + g)).then_inc(s_.s_out, 1)
            for g in range(2):
                dve.wait_ge(s_.vn1, g + 1)
                dve.tensor_copy(VN[:, 8 + 4 * g:12 + 4 * g], four(4 + g)).then_inc(s_.vn1_out, 1)
            for u in range(4):
                dve.wait_ge(s_.o_done, u + 1)
                dve.tensor_copy(OD[:, 2 * u:2 * u + 2], two(PS[:, OB[u], :])).then_inc(s_.o_out, 1)
            dve.wait_ge(s_.zg_done, 1)
            for u in range(4):
                blk = slice(2 * u, 2 * u + 2)
                dve.wait_ge(s_.osq, u + 1)
                dve.tensor_tensor(OD[:, blk], OD[:, blk], ZS[:, blk], ALU.mult).then_inc(s_.gated, 1)
            dve.wait_ge(s_.osd, 1)
            dve.reciprocal(RNC[:, 0:16], RNS[:, 0:16]).then_inc(s_.rnc, 1)
            for u in range(4):
                blk = slice(2 * u, 2 * u + 2)
                dve.wait_ge(s_.gated, u + 1)
                dve.wait_ge(s_.orows, u + 1)
                dve.tensor_tensor(OD[:, blk], OD[:, blk], two(PS[:, RB[u], :]), ALU.mult).then_inc(s_.on2, 1)
            for u in range(4):
                blk = slice(2 * u, 2 * u + 2)
                dve.wait_ge(s_.oo, u + 1)
                dve.tensor_tensor(DOL[:, blk], OD[:, blk], DOH[:, blk].bitcast(F32), ALU.subtract).then_inc(s_.yy, 1)
            dve.wait_ge(s_.h2, 1)
            residual("do", 3)

            def mlp(layer):
                def square(st):
                    split_lo(dve, st)
                    if st.i is None and st.j == 2:
                        norm_scale(dve, ch, 3 + 2 * layer)
                    dve.wait_ge(freed[st.slot], st.uses())
                    dve.tensor_tensor(HP[:, st.slot], SG[:, st.slot], SG[:, st.slot], ALU.mult).then_inc(s_.hp_done, 1)
                    if st.i is not None or st.j:
                        hidden_lo(dve, st, 2, HBASE[f"u{layer}"])
                u = seg[f"u{layer}"]
                steps(dve, u, square, head=3)
                hidden_lo(dve, Step(u, u.n, None), 2, HBASE[f"u{layer}"])
                w = seg[f"w{layer}"]
                row_chunks(w, 4 + 2 * layer)

            mlp(0)
            for t in range(12):
                st = moba_step(t)
                pair = 8 + (t - 3) // 2 if 3 <= t <= 9 and t % 2 else None
                if pair:
                    attn_shift(dve, ch, pair)
                split_lo(dve, st)
                if t == 0:
                    norm_scale(dve, ch, 4)
                if pair:
                    attn_scale(dve, ch, pair)
                if t < 8:
                    read_out(st, QK[:, (t % 2) * 8 + (t // 2) * 2:(t % 2) * 8 + (t // 2) * 2 + 2])
                else:
                    read_v(st)
                if t >= 10:
                    attn_ol(dve, 8 + t - 10)
            attn_ol(dve, 10)
            attn_ol(dve, 11)
            residual("mo", 5)
            mlp(1)
            dve.wait_ge(s_.sd_done, FINAL + 2)
            ch(dve.reciprocal(RSTD[:], RH[:]))
            ch.wait(dve)
            for p in range(4):
                for j in (2 * p, 2 * p + 1):
                    ins = dve.scalar_tensor_tensor(out=XN[:, j], in0=H[:, j], scalar=weight(FINAL, j), in1=RSTD[:],
                                                   op0=ALU.mult, op1=ALU.mult)
                ins.then_inc(s_.xout, 1)

        @block.tensor
        def _(pe):
            def times_x(m, tokens_out=False):
                def body(st):
                    if st.i is not None:
                        return multiply(pe, st, XH, XL, None, tokens_out)
                    multiply(pe, st, XH, XL, None if st.j else (s_.xl_ready, 4 * m), tokens_out,
                             between=lambda: norm_point(pe, m, 2 * st.j))
                    norm_point(pe, m, 2 * st.j + 1)
                return body

            def qk(st):
                if st.i is None and st.j == 1:
                    pe.wait_ge(s_.const, 2)
                times_x(0)(st)
                if st.i is None and st.j == 2:
                    pe.wait_ge(s_.bias_masked, 1)
                    pe.wait_ge(s_.flip_ready, 1)
                    for n in range(8):
                        if n >= 2:
                            pe.wait_ge(s_.bias_ready, n - 1)
                        pe.matmul(two(PS[:, 6 + n % 2, :]), FLIP[:], BREV[:, 2 * n:2 * n + 2], start=True, stop=True).then_inc(s_.bias_turned, 1)
            steps(pe, seg["qk"], qk, head=SLOTS)
            steps(pe, seg["v"], lambda st: multiply(pe, st, XH, XL, tokens_out=True))
            c = seg["xg"].first - 1
            pe.wait_ge(freed[c % SLOTS], c // SLOTS + 1)
            attn_scores(pe, 0)
            for st in (Step(seg["xg"], j, None) for j in range(8)):
                multiply(pe, st, XH, XL)
                if st.j:
                    attn_pv(pe, st.j - 1)
                attn_turn(pe, st.j)
                if st.j < 7:
                    attn_scores(pe, st.j + 1)
            pe.wait_ge(s_.wri_in, 64)
            for st in (Step(seg["gab"], j, None) for j in range(8)):
                j = st.j
                multiply(pe, st, XH, XL)
                if j == 0:
                    attn_pv(pe, 7)
                pe.wait_ge(s_.conv_done, j + 1)
                if j >= 2:
                    pe.wait_ge(s_.gates_done, 2 * j - 2)
                for r in range(2):
                    mm = pe.matmul(PS[:, 3 + j % 2, r * TOK:(r + 1) * TOK], WRI[:, r, j], XN[:, j], start=True, stop=True)
                mm.then_inc(s_.rg_done, 1)
            pe.wait_ge(s_.ol_done, 8)
            steps(pe, seg["ao"], lambda st: multiply(pe, st, OH, OL))
            steps(pe, seg["ro"], lambda st: multiply(pe, st, XH, XL, (s_.y_done, 0) if st.j == 0 else None))
            steps(pe, seg["wo"], lambda st: multiply(pe, st, OH, OL, (s_.ml_done, 0) if st.j == 0 else None))
            steps(pe, seg["fi"], times_x(1), head=2)
            banks_free(pe, seg["fo"])
            steps(pe, seg["fo"], lambda st: multiply_rows(pe, st, st.local(0, 2)), head=1, tail=1)

            def four(b):
                return PS[:, b, :].rearrange("p (n i) -> p n i", n=4)

            def rows_of(t, first, b):
                for e in range(4):
                    mm = pe.transpose(four(b)[:, e], t[:, first + e:first + e + 1].to_broadcast([P, P]), IDENT[:])
                return mm

            def decay_rows(g):
                if g >= 2:
                    pe.wait_ge(s_.b_read, g - 1)
                pe.wait_ge(s_.gc_done, 1)
                rows_of(GC, 4 * g, 6 + g % 2).then_inc(s_.b_done, 1)

            def dq(st):
                if st.i is None and st.j == 9:
                    for g in range(2):
                        decay_rows(g)
                times_x(2)(st)
                if st.i is None and st.j >= 10:
                    decay_rows(st.j - 8)
                if st.i is None and st.j == 1:
                    for c in range(TT):
                        for k in range(KB):
                            mm = pe.matmul(PS[:, 3, 256 + 16 * c:272 + 16 * c], H[:, k, c * P:(c + 1) * P], WBA[:, k],
                                           start=(k == 0), stop=(k == KB - 1))
                    mm.then_inc(s_.ba_done, 1)
                if st.i is None and st.j == 2:
                    pe.wait_ge(s_.g_ready, 1)
                    pe.matmul(PS[:, 3, 320:336], TRI[:], GT[:], start=True, stop=True).then_inc(s_.gc_sum, 1)
            steps(pe, seg["dq"], dq, head=3, tail=3)
            for st in (Step(seg["dz"], j, None) for j in range(4)):
                multiply(pe, st, XH, XL)
                if st.j in (1, 2):
                    u = st.j - 1
                    pe.wait_ge(s_.l2sq, u + 1)
                    for n in range(16):
                        sq = (SQK, XN)[u][:, n % 8, (n // 8) * P:(n // 8) * P + P]
                        mm = pe.matmul(PS[:, 4 + u, n:n + 1], sq, ONES[:, 0:1], start=True, stop=True)
                    mm.then_inc(s_.l2sum, 1)

            def tok(block_, n):
                return QKV[:, block_ + n % 8, (n // 8) * P:(n // 8) * P + P]

            for g in range(4):
                pe.wait_ge(s_.rnc, 1)
                pe.wait_ge(s_.dt_ready, 8)
                rows_of(RNC, 4 * g, UB[g]).then_inc(s_.unit_rows, 1)
            for k in range(SLOTS):
                pe.wait_ge(freed[k], uses_upto(seg["dz"], k))
            for g in range(4):
                pe.wait_ge(s_.rnc, 2)
                rows_of(RNC, 16 + 4 * g, UB[4 + g]).then_inc(s_.unit_rows, 1)
            for g in range(4):
                pe.wait_ge(s_.l2done, g + 1)
                for e in range(4):
                    n = 4 * g + e
                    mm = pe.matmul(four(UB[g])[:, e], tok(8, n), tok(8, n), start=True, stop=True)
                mm.then_inc(s_.gk_done, 1)
            def turn_c(g):
                pe.wait_ge(s_.c_done, g + 1)
                for e in range(4):
                    mm = pe.transpose(four(UB[g])[:, e], CM[:, 4 * g + e], IDENT[:])
                mm.then_inc(s_.ct_done, 1)

            for g in range(4):
                pe.wait_ge(s_.l2done, g + 5)
                for e in range(4):
                    n = 4 * g + e
                    mm = pe.matmul(four(UB[4 + g])[:, e], tok(8, n), tok(0, n), start=True, stop=True)
                mm.then_inc(s_.kq_done, 1)
                if g:
                    turn_c(g - 1)
            turn_c(3)

            def level_p1(n):
                g = n % 4
                pe.wait_ge(s_.c_done, n + 5)
                if n < 2:
                    pe.wait_ge(s_.at_done, 2)
                    pe.wait_ge(s_.ty_out, n + 1)
                else:
                    pe.wait_ge(s_.ty_out, n + 1)
                    pe.wait_ge(s_.p1_out, n - 1)
                for e in range(4):
                    mm = pe.matmul(four(n % 2)[:, e], CM[:, 4 * g + e], TY[:, 4 * g + e], start=True, stop=True)
                mm.then_inc(s_.p1_done, 1)

            def level_q(n):
                g = n % 4
                pe.wait_ge(s_.p1_out, n + 1)
                if n < 4:
                    pe.wait_ge(s_.tx_in, n + 1)
                else:
                    pe.wait_ge(s_.x_out, n - 3)
                if n >= 2:
                    pe.wait_ge(s_.ty_out, n + 3)
                else:
                    pe.wait_ge(s_.ty_out, 2)
                    pe.wait_ge(s_.at_done, 4)
                for e in range(4):
                    i = 4 * g + e
                    mm = pe.matmul(four(4 + n % 2)[:, e], TX[:, i], P1[:, i], start=True, stop=True)
                mm.then_inc(s_.q_done, 1)

            def level_x(n):
                g = n % 4
                pe.wait_ge(s_.ty_out, n + 5)
                if n >= 2:
                    pe.wait_ge(s_.x_out, n - 1)
                for e in range(4):
                    mm = pe.transpose(four(2 + n % 2)[:, e], TY[:, 4 * g + e], IDENT[:])
                mm.then_inc(s_.x_done, 1)

            def turn(u):
                if u >= 2:
                    pe.wait_ge(s_.vt_out, u - 1)
                else:
                    pe.wait_ge(s_.ty_out, 3 + u)
                if u >= 8:
                    pe.wait_ge(s_.sm_ready, 4)
                    return rows_of(EGC, 4 * (u - 6), 6 + u % 2).then_inc(s_.tr_done, 1)
                for e in range(4):
                    n = 4 * (u % 4) + e
                    mm = pe.transpose(four(6 + u % 2)[:, e], tok(16 if u < 4 else 8, n), IDENT[:])
                mm.then_inc(s_.tr_done, 1)

            for n in range(24):
                level_p1(n)
                if n:
                    level_q(n - 1)
                if 2 <= n < 22:
                    level_x(n - 2)
                if n < 10:
                    turn(n)
            level_q(23)
            for g in range(2):
                pe.wait_ge(s_.ty_out, 4 + 20 + g + 1)
                pe.wait_ge(s_.vt_out, 10)
                for e in range(4):
                    n = 4 * g + e
                    mm = pe.matmul(four(6 + g)[:, e], TY[:, n], VB[:, n], start=True, stop=True)
                mm.then_inc(s_.vn0, 1)
            for g in range(2):
                pe.wait_ge(s_.ty_out, 4 + 20 + g + 3)
                for e in range(4):
                    n = 4 * g + e
                    mm = pe.matmul(four(g)[:, e], KBT[:, n], TY[:, 8 + n], start=True, stop=True)
                mm.then_inc(s_.w_done, 1)
            for g in range(2):
                pe.wait_ge(s_.vn0_out, g + 1)
                pe.wait_ge(s_.x_out, 20)
                for e in range(4):
                    n = 4 * g + e
                    mm = pe.matmul(four(2 + g)[:, e], KD[:, n], VN[:, n], start=True, stop=True)
                mm.then_inc(s_.s_done, 1)
            for g in range(2):
                pe.wait_ge(s_.s_out, g + 1)
                pe.wait_ge(s_.w_out, g + 1)
                for e in range(4):
                    n = 4 * g + e
                    pe.matmul(four(4 + g)[:, e], TY[:, 8 + n], VB[:, 8 + n], start=True, stop=False, skip_group_check=True)
                    mm = pe.matmul(four(4 + g)[:, e], NW[:, n], ST[:, n], start=False, stop=True, skip_group_check=True)
                mm.then_inc(s_.vn1, 1)
            for u in range(4):
                pe.wait_ge(s_.vn1_out, u // 2 + 1)
                for e in range(2):
                    h = 2 * u + e
                    out = PS[:, OB[u], e * TOK:(e + 1) * TOK]
                    pe.matmul(out[:, 0:P], VN[:, h], AT[:, h], start=True, stop=True, skip_group_check=True)
                    pe.matmul(out[:, P:TOK], VN[:, 8 + h], AT[:, 8 + h], start=True, stop=False, skip_group_check=True)
                    mm = pe.matmul(out[:, P:TOK], ST[:, h], QKV[:, h, P:TOK], start=False, stop=True, skip_group_check=True)
                mm.then_inc(s_.o_done, 1)
            for u in range(4):
                pe.wait_ge(s_.osq, u + 1)
                for h in (2 * u, 2 * u + 1):
                    for c in range(TT):
                        mm = pe.matmul(PS[:, 4, 8 * c + h:8 * c + h + 1], OSQ[:, h, c * P:(c + 1) * P], ONES[:, 0:1], start=True, stop=True)
            mm.then_inc(s_.osum, 1)
            pe.wait_ge(s_.rnc, 3)
            for u in range(4):
                for e in range(2):
                    for c in range(TT):
                        at_, n = e * TOK + c * P, 8 * c + 2 * u + e
                        mm = pe.transpose(PS[:, RB[u], at_:at_ + P], RNC[:, n:n + 1].to_broadcast([P, P]), IDENT[:])
                mm.then_inc(s_.orows, 1)
            steps(pe, seg["do"], lambda st: multiply(pe, st, DOH, DOL, (s_.yy, 0) if st.j == 0 else None))

            def mlp(layer):
                steps(pe, seg[f"u{layer}"], times_x(3 + 2 * layer), head=3)
                w = seg[f"w{layer}"]
                banks_free(pe, w)
                steps(pe, w, lambda st: multiply_rows(pe, st, st.local(HBASE[f"u{layer}"])), head=1, tail=1)

            mlp(0)
            pe.wait_ge(s_.const, 3)
            for t in range(12):
                st = moba_step(t)
                multiply(pe, st, XH, XL, None if t else (s_.xl_ready, 16), tokens_out=t >= 8,
                         between=lambda: norm_point(pe, 4, 2 * t))
                norm_point(pe, 4, 2 * t + 1)
                if 3 <= t <= 9 and t % 2:
                    attn_turn(pe, 8 + (t - 3) // 2)
                if 2 <= t <= 8 and t % 2 == 0:
                    c = seg["mq"].first + t - 1
                    pe.wait_ge(freed[c % SLOTS], c // SLOTS + 1)
                    attn_scores(pe, 8 + (t - 2) // 2)
                if t >= 9:
                    c = seg["mv"].first + t - 9
                    pe.wait_ge(freed[c % SLOTS], c // SLOTS + 1)
                    attn_pv(pe, 8 + t - 9)
            c = seg["mv"].first + 3
            pe.wait_ge(freed[c % SLOTS], c // SLOTS + 1)
            attn_pv(pe, 11)
            steps(pe, seg["mo"], lambda st: multiply(pe, st, OH, OL, None if st.j else (s_.ol_done, 8)))
            mlp(1)
            norm_sums(pe, FINAL)


_VECTORS = [name for name, _ in VECTORS]


def kernel(**inputs):
    import numpy as np
    import concourse.bacc as bacc
    from concourse.bass_utils import run_bass_kernel_spmd

    x = {k: np.asarray(v) for k, v in inputs.items()}

    def columns(v):
        return np.ascontiguousarray(v.reshape(-1, P).T)

    arrays = {
        "x": np.ascontiguousarray(x["x"][0].T),
        "vectors": np.concatenate([columns(x[n]) for n in _VECTORS], axis=1),
        "rel_reversed": np.ascontiguousarray(x["rel_table"][0][:, ::-1]),
        "dn_a_log": x["dn_a_log_2"], "dn_dt_bias": x["dn_dt_bias_2"],
        "w_in": x["w_in"][0], "w_rg_r": x["w_rg_r"][0], "w_rg_i": x["w_rg_i"][0],
        "w_attn_out": x["w_attn_out"][0], "w_rnn_out": x["w_rnn_out"][0], "w_o": x["w_o"][0],
        "w_ffn_in_pairs": x["w_ffn_in"][0].reshape(D, 2, FF1 // P, P).transpose(0, 2, 1, 3).reshape(D, 2 * FF1),
        "w_ffn_out": x["w_ffn_out"][0],
        "dn_w_in": x["dn_w_in_2"][0], "dn_w_out": x["dn_w_out_2"][0],
        "mb_w_in": x["mb_w_in_2"][0], "mb_w_out": x["mb_w_out_2"][0],
        "mlp_w_up": x["mlp_w_up_2"], "mlp_w_down": x["mlp_w_down_2"],
    }
    nc = bacc.Bacc("TRN2", target_bir_lowering=False, num_devices=1)
    maps, aps = {}, {}
    for name, v in arrays.items():
        v = np.ascontiguousarray(v)
        maps[f"in_{name}"] = v
        aps[name] = nc.dram_tensor(f"in_{name}", v.shape, mybir.dt.from_np(v.dtype), kind="ExternalInput").ap()
    aps["out"] = nc.dram_tensor("out_t", (D, TOK), F32, kind="ExternalOutput").ap()
    build(nc, aps)
    r = run_bass_kernel_spmd(nc, [maps], core_ids=[0])
    return np.ascontiguousarray(r.results[0]["out_t"].T)[None]
```
